# Optimizing a Trainium2 kernel written in Bass

```python
import math
import jax, jax.numpy as jnp
from jax import lax
import numpy as np

D_MODEL = 1024
BATCH = 1
SEQ = 512
DEPTH = 2

CHUNK = 64
N_MIXERS = 3
N_FOX = len(range(0, DEPTH, N_MIXERS))
N_SWA = len(range(1, DEPTH, N_MIXERS))
N_RWKV = len(range(2, DEPTH, N_MIXERS))
HEAD_DIM = 64
FOX_HEADS = D_MODEL // HEAD_DIM
FOX_QBLOCK = 128
SWA_Q_HEADS = D_MODEL // HEAD_DIM
SWA_GROUP = 8
SWA_KV_HEADS = SWA_Q_HEADS // SWA_GROUP
SWA_WINDOW = 128
SWA_BAND = SWA_WINDOW // CHUNK
SWA_QKV = (SWA_Q_HEADS + 2 * SWA_KV_HEADS) * HEAD_DIM
RWKV_HEADS = D_MODEL // HEAD_DIM
RWKV_DECAY_LORA = 64
RWKV_A_LORA = 64
RWKV_GATE_LORA = 128
RWKV_GN_EPS = 64e-5
D_FF = 2816
RMS_EPS = 1e-6

kernel_name = "hybrid_fox_swa_rwkv7_macaron"

F32 = jnp.float32

def rms_norm(x, g):
    xf = x.astype(F32)
    y = xf * lax.rsqrt(jnp.mean(xf * xf, axis=-1, keepdims=True) + RMS_EPS)
    return (y * g.astype(F32)).astype(x.dtype)

def swiglu(x, w_in, w_out):
    gate, up = jnp.split(x @ w_in, 2, axis=-1)
    return (jax.nn.silu(gate) * up) @ w_out

def fox_mixer(x, w_in, b_f, w_o):
    B, T, D = x.shape
    H, Dh, QB = FOX_HEADS, HEAD_DIM, FOX_QBLOCK
    proj = x @ w_in
    q, k, v, f_logit = jnp.split(proj, [D, 2 * D, 3 * D], axis=-1)
    to_heads = lambda t: t.reshape(B, T, H, Dh).transpose(0, 2, 1, 3)
    q, k, v = to_heads(q), to_heads(k), to_heads(v)
    log_f = jax.nn.log_sigmoid((f_logit + b_f).astype(F32))
    c = jnp.cumsum(log_f, axis=1).transpose(0, 2, 1)
    nb = T // QB
    q_blocks = q.reshape(B, H, nb, QB, Dh).transpose(2, 0, 1, 3, 4)
    c_blocks = c.reshape(B, H, nb, QB).transpose(2, 0, 1, 3)
    q_pos = jnp.arange(T).reshape(nb, QB)
    k_pos = jnp.arange(T)
    scale = HEAD_DIM ** -0.5

    def block(args):
        qb, cb, pb = args
        s = jnp.einsum('bhqd,bhkd->bhqk', qb, k, preferred_element_type=F32) * scale
        s = s + cb[..., None] - c[:, :, None, :]
        s = jnp.where(pb[:, None] >= k_pos[None, :], s, -jnp.inf)
        p = jax.nn.softmax(s, axis=-1)
        return jnp.einsum('bhqk,bhkd->bhqd', p.astype(v.dtype), v)

    o = lax.map(block, (q_blocks, c_blocks, q_pos))
    o = o.transpose(1, 0, 3, 2, 4).reshape(B, T, D)
    return (o @ w_o).astype(x.dtype)

def swa_mixer(x, w_in, b_in, sinks, w_o):
    B, T, D = x.shape
    Hkv, G, Dh = SWA_KV_HEADS, SWA_GROUP, HEAD_DIM
    proj = x @ w_in + b_in
    q, k, v = jnp.split(proj, [SWA_Q_HEADS * Dh, (SWA_Q_HEADS + Hkv) * Dh], axis=-1)
    nc = T // CHUNK
    q = q.reshape(B, nc, CHUNK, Hkv, G, Dh)
    k = k.reshape(B, nc, CHUNK, Hkv, Dh)
    v = v.reshape(B, nc, CHUNK, Hkv, Dh)

    def band(t):
        padded = jnp.pad(t, ((0, 0), (SWA_BAND - 1, 0), (0, 0), (0, 0), (0, 0)))
        return jnp.concatenate([padded[:, j:j + nc] for j in range(SWA_BAND)], axis=2)

    kb, vb = band(k), band(v)
    key_chunk = (jnp.arange(nc)[:, None] + (jnp.arange(SWA_BAND * CHUNK) // CHUNK)[None, :]
                 - (SWA_BAND - 1))
    valid = (key_chunk >= 0)[None, :, None, None, None, :]
    s = jnp.einsum('bnqhgd,bnkhd->bnhgqk', q, kb, preferred_element_type=F32) * (Dh ** -0.5)
    s = jnp.where(valid, s, -jnp.inf)
    sink = sinks.astype(F32).reshape(Hkv, G)[None, None, :, :, None, None]
    m = jnp.maximum(jnp.max(s, axis=-1, keepdims=True), sink)
    p = jnp.exp(s - m)
    p = p / (jnp.sum(p, axis=-1, keepdims=True) + jnp.exp(sink - m))
    o = jnp.einsum('bnhgqk,bnkhd->bnqhgd', p.astype(vb.dtype), vb).reshape(B, T, D)
    return (o @ w_o).astype(x.dtype)

def rwkv7_mixer(x, mu, w_rkv, w0, w1, w2, a0, a1, a2, g1, g2, k_k, k_a, r_k, gn_w, gn_b, w_o):
    B, T, D = x.shape
    H, N = RWKV_HEADS, HEAD_DIM
    xx = jnp.pad(x, ((0, 0), (1, 0), (0, 0)))[:, :-1] - x
    mix = lambda i: x + xx * mu[i]
    xrkv = jnp.stack([mix(0), mix(1), mix(2)])
    r, k, v = jnp.einsum('pbtd,pde->pbte', xrkv, w_rkv)
    xw, xa, xg = mix(3), mix(4), mix(5)
    w_log = -jax.nn.softplus(-(w0 + jnp.tanh(xw @ w1) @ w2).astype(F32)) - 0.5
    decay = jnp.exp(-jnp.exp(w_log))
    a = jax.nn.sigmoid((a0 + (xa @ a1) @ a2).astype(F32))
    g = jax.nn.sigmoid(xg @ g1) @ g2
    r, k, v = r.astype(F32), k.astype(F32), v.astype(F32)
    kk = (k * k_k.astype(F32)).reshape(B, T, H, N)
    kk = kk / jnp.maximum(jnp.sqrt(jnp.sum(kk * kk, axis=-1, keepdims=True)), 1e-12)
    k = k * (1.0 + (a - 1.0) * k_a.astype(F32))
    heads = lambda t: t.reshape(B, T, H, N)
    rh, kh, vh, ah, wh = heads(r), heads(k), heads(v), heads(a), heads(decay)
    a_vec, b_vec = -kk, kk * ah
    to_time = lambda t: jnp.moveaxis(t, 1, 0)

    def step(S, inp):
        rt, wt, kt, vt, at, bt = inp
        sa = jnp.einsum('bhvk,bhk->bhv', S, at)
        S = S * wt[:, :, None, :] + sa[..., None] * bt[:, :, None, :] + vt[..., None] * kt[:, :, None, :]
        return S, jnp.einsum('bhvk,bhk->bhv', S, rt)

    S0 = jnp.zeros((B, H, N, N), F32)
    _, y = lax.scan(step, S0, tuple(to_time(t) for t in (rh, wh, kh, vh, a_vec, b_vec)))
    y = jnp.moveaxis(y, 0, 1)
    mean = jnp.mean(y, axis=-1, keepdims=True)
    var = jnp.mean(jnp.square(y - mean), axis=-1, keepdims=True)
    y = (y - mean) * lax.rsqrt(var + RWKV_GN_EPS)
    y = y * gn_w.astype(F32).reshape(H, N) + gn_b.astype(F32).reshape(H, N)
    y = y + jnp.sum(rh * kh * r_k.astype(F32), axis=-1, keepdims=True) * vh
    y = y.reshape(B, T, D).astype(x.dtype) * g
    return (y @ w_o).astype(x.dtype)

def setup_inputs(seed: int = 0) -> dict:
    key = jax.random.key(seed)
    ks = iter(jax.random.split(key, 32))
    nrm = lambda shape, s: jax.random.normal(next(ks), shape, F32) * s
    uni = lambda shape, lo, hi: jax.random.uniform(next(ks), shape, F32, lo, hi)
    D, H = D_MODEL, FOX_HEADS
    return {
        "x": nrm((BATCH, SEQ, D), 1.0),
        "norm_g": 1.0 + nrm((DEPTH, 3, D), 0.02),
        "ffn_w_in": nrm((DEPTH, 2, D, 2 * D_FF), D ** -0.5),
        "ffn_w_out": nrm((DEPTH, 2, D_FF, D), D_FF ** -0.5),
        "fox_w_in": nrm((N_FOX, D, 3 * D + H), D ** -0.5),
        "fox_b_f": uni((N_FOX, H), 1.0, 4.0),
        "fox_w_o": nrm((N_FOX, D, D), D ** -0.5),
        "swa_w_in": nrm((N_SWA, D, SWA_QKV), D ** -0.5),
        "swa_b_in": nrm((N_SWA, SWA_QKV), 0.02),
        "swa_sinks": nrm((N_SWA, SWA_Q_HEADS), 1.0),
        "swa_w_o": nrm((N_SWA, D, D), D ** -0.5),
        "rwkv_mu": uni((N_RWKV, 6, D), 0.0, 1.0),
        "rwkv_w_rkv": nrm((N_RWKV, 3, D, D), D ** -0.5),
        "rwkv_w0": uni((N_RWKV, D), -6.0, -1.0),
        "rwkv_w1": nrm((N_RWKV, D, RWKV_DECAY_LORA), 0.1 * D ** -0.5),
        "rwkv_w2": nrm((N_RWKV, RWKV_DECAY_LORA, D), 0.1 * RWKV_DECAY_LORA ** -0.5),
        "rwkv_a0": nrm((N_RWKV, D), 0.1),
        "rwkv_a1": nrm((N_RWKV, D, RWKV_A_LORA), D ** -0.5),
        "rwkv_a2": nrm((N_RWKV, RWKV_A_LORA, D), 0.5 * RWKV_A_LORA ** -0.5),
        "rwkv_g1": nrm((N_RWKV, D, RWKV_GATE_LORA), D ** -0.5),
        "rwkv_g2": nrm((N_RWKV, RWKV_GATE_LORA, D), RWKV_GATE_LORA ** -0.5),
        "rwkv_k_k": 0.85 + nrm((N_RWKV, D), 0.05),
        "rwkv_k_a": 1.0 + nrm((N_RWKV, D), 0.05),
        "rwkv_r_k": nrm((N_RWKV, RWKV_HEADS, HEAD_DIM), 0.1),
        "rwkv_gn_w": 1.0 + nrm((N_RWKV, D), 0.02),
        "rwkv_gn_b": nrm((N_RWKV, D), 0.02),
        "rwkv_w_o": nrm((N_RWKV, D, D), D ** -0.5),
        "final_g": 1.0 + nrm((D,), 0.02),
    }

def reference(x, norm_g, ffn_w_in, ffn_w_out, fox_w_in, fox_b_f, fox_w_o,
              swa_w_in, swa_b_in, swa_sinks, swa_w_o,
              rwkv_mu, rwkv_w_rkv, rwkv_w0, rwkv_w1, rwkv_w2, rwkv_a0, rwkv_a1, rwkv_a2,
              rwkv_g1, rwkv_g2, rwkv_k_k, rwkv_k_a, rwkv_r_k, rwkv_gn_w, rwkv_gn_b, rwkv_w_o,
              final_g):
    h = x
    for i in range(DEPTH):
        kind, j = i % N_MIXERS, i // N_MIXERS
        h = h + 0.5 * swiglu(rms_norm(h, norm_g[i, 0]), ffn_w_in[i, 0], ffn_w_out[i, 0])
        u = rms_norm(h, norm_g[i, 1])
        if kind == 0:
            m = fox_mixer(u, fox_w_in[j], fox_b_f[j], fox_w_o[j])
        elif kind == 1:
            m = swa_mixer(u, swa_w_in[j], swa_b_in[j], swa_sinks[j], swa_w_o[j])
        else:
            m = rwkv7_mixer(u, rwkv_mu[j], rwkv_w_rkv[j], rwkv_w0[j], rwkv_w1[j], rwkv_w2[j],
                            rwkv_a0[j], rwkv_a1[j], rwkv_a2[j], rwkv_g1[j], rwkv_g2[j],
                            rwkv_k_k[j], rwkv_k_a[j], rwkv_r_k[j], rwkv_gn_w[j], rwkv_gn_b[j],
                            rwkv_w_o[j])
        h = h + m
        h = h + 0.5 * swiglu(rms_norm(h, norm_g[i, 2]), ffn_w_in[i, 1], ffn_w_out[i, 1])
    return rms_norm(h, final_g)


_drawn_inputs = setup_inputs


def setup_inputs(seed=0):
    import zlib

    import numpy as np

    out = dict(_drawn_inputs(seed))
    spreads = {}
    factors = {'norm_g': 2.794, 'swa_b_in': 3.353, 'swa_sinks': 8.0, 'final_g': 3.119}
    for name, (base, spread) in spreads.items():
        noise = np.random.default_rng([zlib.crc32(name.encode()), seed]).standard_normal(out[name].shape)
        drawn = base * np.exp(spread * noise) if base else spread * noise
        out[name] = __import__('jax').numpy.asarray(drawn.astype(out[name].dtype))
    for name, factor in factors.items():
        out[name] = (out[name] * factor).astype(out[name].dtype)
    return out
```

```python
from contextlib import ExitStack

import numpy as np

import concourse.bass as bass
from concourse import mybir

F32 = mybir.dt.float32
F32R = mybir.dt.float32r
BF16 = mybir.dt.bfloat16
ALU = mybir.AluOpType
ACT = mybir.ActivationFunctionType
AX_X = mybir.AxisListType.X

P = 128
SEQ = 512
D = 1024
DFF = 2816
HEADS = 16
DH = 64
KV_HEADS = 2
TB = SEQ // P
KB = D // P
FB = DFF // P
PAIRS = HEADS // 2
RMS_EPS = 1e-6
QSCALE = DH ** -0.5
MASKED = -1e30

RAW = 4
SPLIT = 2
UNIT = 1024
LOOK = SPLIT

IN_BODIES = FB // 2
IN_UNITS = 4
OUT_KBS = [range(3 * u, 3 * u + 3) for u in range(6)] + [range(18, 20), range(20, 22)]
OUT_COLS = 3 * 256
OUT_BODIES = 2
WO_KBS = [range(0, 4), range(4, 8)]

FFN_UNITS = IN_BODIES * IN_UNITS + (KB // 2) * len(OUT_KBS)
WO_UNITS = (KB // 2) * len(WO_KBS)
V_UNITS = 8
FOX_UNITS = 1 + V_UNITS + 2 * PAIRS + WO_UNITS
SWA_UNITS = 2 + PAIRS + WO_UNITS
FFN_BASE = [0, FFN_UNITS + FOX_UNITS, 2 * FFN_UNITS + FOX_UNITS, 3 * FFN_UNITS + FOX_UNITS + SWA_UNITS]
MIX_BASE = [FFN_UNITS, 3 * FFN_UNITS + FOX_UNITS]
TOTAL_UNITS = 4 * FFN_UNITS + FOX_UNITS + SWA_UNITS


class Mixer:

    def __init__(self, n):
        self.n = n
        self.fox = n == 0
        self.base = MIX_BASE[n]
        self.first_key = [0 if self.fox else max(0, i - 1) for i in range(TB)]
        self.keys = [(i + 1 - self.first_key[i]) * P for i in range(TB)]
        self.bank = [2, 2, 3, 4]
        self.bank_at = [0, P, 0, 0]
        self.p_at = [sum(self.keys[:i]) for i in range(TB)]
        self.p_cols = sum(self.keys)

    def queries(self, kb):
        return [i for i in range(TB) if self.first_key[i] <= kb <= i]

    def qk_ready(self, j):
        return 2 * j + 2 if self.fox else 2 * PAIRS + 2 + j


ORDER = (3, 2, 0, 1)


def build(nc, x, gains, final_g, ffn_in, ffn_out, mix_w, fox_b, swa_bq, swa_bk, swa_bv, sinks, y):
    ctx = ExitStack()
    with ctx:
        def sb(name, shape, dt=F32):
            return ctx.enter_context(nc.sbuf_tensor(name, shape, dt))

        def sem(name):
            return ctx.enter_context(nc.semaphore(name))

        h = sb("h", [P, KB * SEQ])
        u_hi = sb("u_hi", [P, KB * SEQ], F32R)
        u_lo = sb("u_lo", [P, KB * SEQ], F32R)
        wide_hi = sb("wide_hi", [P, 12288], F32R)
        wide_lo = sb("wide_lo", [P, 12288], F32R)
        V_AT, O_AT, PT_AT, K_AT, QA_AT, QB_AT = 0, 4096, 8192, 9216, 10240, 11264
        raw = sb("raw", [P, RAW, UNIT])
        w_hi = sb("w_hi", [P, SPLIT, UNIT], F32R)
        w_lo = sb("w_lo", [P, SPLIT, UNIT], F32R)
        scratch = sb("scratch", [P, 6 * SEQ])
        final_gb = sb("final_gb", [P, D])
        rstd_row = sb("rstd_row", [P, SEQ])
        sq = sb("sq", [P, 2, SEQ])
        acc = sb("acc", [P, SEQ])
        diag = sb("diag", [P, SEQ])
        gain = sb("gain", [P, 6 * KB])
        ident = sb("ident", [P, P])
        ones = sb("ones", [P, P])
        ident_bf = sb("ident_bf", [P, P], BF16)
        mask = sb("mask", [P, 2, 2, P], BF16)
        ms = sb("ms", [P, TB])
        half = sb("half", [P, TB])
        rstd = sb("rstd", [P, TB])
        bf = sb("bf", [HEADS, 1])
        bq = sb("bq", [P, PAIRS])
        bk = sb("bk", [P, 1])
        bv = sb("bv", [P, KV_HEADS * DH])
        sink = sb("sink", [P, HEADS])
        nsink = sb("nsink", [P, HEADS])
        nmax = sb("nmax", [P, 2, TB])
        psum_p = sb("psum_p", [P, 2, TB])
        esink = sb("esink", [P, 2, TB])
        rsum = sb("rsum", [P, 2, TB])
        pick = sb("pick", [P, HEADS])
        pick_r = sb("pick_r", [P, HEADS], F32R)
        decay = sb("decay", [P, SEQ], F32R)
        g_scaled_buf, silu_buf, up_buf = (scratch[:, 2 * n * SEQ:2 * (n + 1) * SEQ] for n in range(3))
        prob = [scratch[:, 0:1280], scratch[:, 1280:2560]]
        scaled = scratch[:, 2560:3072]
        bank = [ctx.enter_context(nc.psum_tensor(f"bank{b}", [P, 512], F32)) for b in range(8)]

        x_loaded = [sem(f"x_loaded{t}") for t in range(TB)]
        small_loaded = sem("small_loaded")
        final_g_loaded = sem("final_g_loaded")
        raw_loaded = [sem(f"raw_loaded{s}") for s in range(RAW)]
        w_hi_ready = sem("w_hi_ready")
        w_ready = sem("w_ready")
        unit_used = sem("unit_used")
        consts = sem("consts")
        consts_pool = sem("consts_pool")
        ident_ready = sem("ident_ready")
        x_turned = sem("x_turned")
        h_ready = sem("h_ready")
        u_hi_ready = sem("u_hi_ready")
        u_ready = sem("u_ready")
        sq_ready = sem("sq_ready")
        acc_ready = sem("acc_ready")
        tok_sum = sem("tok_sum")
        ms_ready = sem("ms_ready")
        rstd_ready = sem("rstd_ready")
        diag_ready = sem("diag_ready")
        row_sum = sem("row_sum")
        row_ready = sem("row_ready")
        gate_scaled = sem("gate_scaled")
        silu_ready = sem("silu_ready")
        up_scaled = sem("up_scaled")
        prod_ready = sem("prod_ready")
        a_hi_ready = sem("a_hi_ready")
        a_ready = sem("a_ready")
        f_chain = sem("f_chain")
        f_act = sem("f_act")
        decay_ready = sem("decay_ready")
        v_scaled = sem("v_scaled")
        v_hi_ready = sem("v_hi_ready")
        v_ready = sem("v_ready")
        zeroed = sem("zeroed")
        qk_raw = sem("qk_raw")
        qk_scaled = sem("qk_scaled")
        qk_hi_ready = sem("qk_hi_ready")
        qk_ready = sem("qk_ready")
        scored = sem("scored")
        maxed = sem("maxed")
        nmax_ready = sem("nmax_ready")
        nsink_ready = sem("nsink_ready")
        expd = sem("expd")
        esink_ready = sem("esink_ready")
        sum_ready = sem("sum_ready")
        rsum_ready = sem("rsum_ready")
        p_ready = sem("p_ready")
        turned = sem("turned")
        pt_hi_ready = sem("pt_hi_ready")
        pt_ready = sem("pt_ready")
        pv_done = sem("pv_done")
        o_hi_ready = sem("o_hi_ready")
        o_ready = sem("o_ready")
        y_turned = sem("y_turned")
        y_scaled = sem("y_scaled")
        y_stored = sem("y_stored")

        block = ctx.enter_context(nc.Block())

        def blk(t, m, n=1):
            return t[:, m * SEQ:(m + n) * SEQ]

        def f32(ap):
            return ap.bitcast(F32)

        def dyn(t, start, size=SEQ):
            return t[:, bass.ds(start, size)]

        @block.sync
        def _(sp):
            x_at = [scratch[:, 0:D], scratch[:, D:2 * D], scratch[:, 2 * D:3 * D], final_gb[:, :]]
            for t in range(TB):
                sp.dma_start(x_at[t], x[t * P:(t + 1) * P, :]).then_inc(x_loaded[t], 16)

            def load(n, slot, src, cols, wait=None):
                if wait is not None:
                    sp.wait_ge(w_ready, wait)
                sp.dma_start(raw[:, slot, 0:cols], src).then_inc(raw_loaded[slot], 16)

            def load_ffn(f):
                base = FFN_BASE[f]

                def load_in(i):
                    for r in range(IN_UNITS):
                        load(r, (base + r) % RAW, ffn_in[f, i, r], UNIT,
                             None if f == 0 and type(i) is int and i == 0 else base + 4 * i + r - RAW + 1)

                load_in(0)
                with sp.Fori(1, IN_BODIES) as i:
                    load_in(i)
                out = base + IN_BODIES * IN_UNITS
                with sp.Fori(0, (KB // 2) * len(OUT_KBS) // RAW) as i:
                    for r in range(RAW):
                        load(r, (out + r) % RAW, ffn_out[f, i, r], OUT_COLS, out + 4 * i + r - RAW + 1)

            def load_mixer(m):
                first = 0 if m.fox else FOX_UNITS
                for n in range(FOX_UNITS if m.fox else SWA_UNITS):
                    load(n, (m.base + n) % RAW, mix_w[first + n], UNIT, m.base + n - RAW + 1)

            load_ffn(0)
            load_mixer(Mixer(0))
            load_ffn(1)
            load_ffn(2)
            load_mixer(Mixer(1))
            load_ffn(3)
            for n in range(2 * TB):
                t, half_d = n % TB, n // TB
                sp.wait_ge(y_scaled, n + 1)
                sp.dma_start(y[t * P:(t + 1) * P, half_d * 512:(half_d + 1) * 512],
                             raw[:, n // 2, (n % 2) * 512:(n % 2 + 1) * 512]).then_inc(y_stored, 16)
            sp.wait_ge(y_stored, 16 * 2 * TB)

        @block.gpsimd
        def _(pool):
            def in_turn(k, ins, s):
                ins.then_inc(s, 1)
                pool.wait_ge(s, k)

            in_turn(1, pool.memset(ones[:, :], 1.0), consts_pool)
            in_turn(2, pool.memset(ident[:, :], 0.0), consts_pool)
            in_turn(3, pool.affine_select(out=ident[:, :], in_=ident[:, :], compare_op=ALU.not_equal, fill=1.0,
                                          base=0, pattern=[[-1, P]], channel_multiplier=1), consts_pool)
            pool.memset(half[:, :], -0.5).then_inc(ident_ready, 1)
            in_turn(4, pool.memset(ident_bf[:, :], 0.0), consts_pool)
            in_turn(5, pool.affine_select(out=ident_bf[:, :], in_=ident_bf[:, :], compare_op=ALU.not_equal,
                                          fill=1.0, base=0, pattern=[[-1, P]], channel_multiplier=1), consts_pool)
            in_turn(6, pool.memset(mask[:, :, :, :], 0.0), consts_pool)
            in_turn(7, pool.affine_select(out=mask[:, 0, 1, :], in_=mask[:, 0, 1, :], compare_op=ALU.is_ge,
                                          fill=MASKED, base=0, pattern=[[-1, P]], channel_multiplier=1), consts_pool)
            in_turn(8, pool.memset(mask[:, 1, 0, 0:64], MASKED), consts_pool)
            in_turn(9, pool.memset(mask[64:128, 1, 0, 64:128], MASKED), consts_pool)
            in_turn(10, pool.memset(mask[0:64, 1, 1, 64:128], MASKED), consts_pool)
            in_turn(11, pool.memset(f32(decay[:, :]), 0.0), consts_pool)
            in_turn(12, pool.memset(pick[:, :], 0.0), consts_pool)
            in_turn(13, pool.affine_select(out=pick[:, :], in_=pick[:, :], compare_op=ALU.not_equal, fill=1.0,
                                           base=0, pattern=[[-1, HEADS]], channel_multiplier=1), consts_pool)
            pool.affine_select(out=pick[:, :], in_=pick[:, :], compare_op=ALU.not_equal, fill=1.0,
                               base=-32, pattern=[[-1, HEADS]], channel_multiplier=1).then_inc(consts, 1)
            pool.wait_ge(consts, 1)

            def pow_rstd(nn):
                pool.wait_ge(ms_ready, nn + 1)
                pool.tensor_tensor(rstd[:, :], ms[:, :], half[:, :], ALU.pow).then_inc(rstd_ready, 1)

            def zero_halves(m):
                pool.wait_ge(unit_used, m.base)
                for k, part in enumerate((wide_hi, wide_lo)):
                    in_turn(4 * m.n + 2 * k + 1, pool.memset(f32(part[64:128, QA_AT:QA_AT + 2 * SEQ]), 0.0), zeroed)
                    in_turn(4 * m.n + 2 * k + 2, pool.memset(f32(part[0:64, QB_AT:QB_AT + 2 * SEQ]), 0.0), zeroed)

            pow_rstd(0)
            zero_halves(Mixer(0))
            pow_rstd(1)
            pow_rstd(2)
            pow_rstd(3)
            zero_halves(Mixer(1))
            pow_rstd(4)
            pow_rstd(5)
            pow_rstd(6)

        @block.tensor
        def _(pe):
            def products(out, pairs, first, last):
                n = 3 * len(pairs)
                k = 0
                for (a_hi, a_lo), (b_hi, b_lo) in pairs:
                    for a, b in ((a_hi, b_hi), (a_hi, b_lo), (a_lo, b_hi)):
                        mm = pe.matmul(out, a, b, start=first and k == 0, stop=last and k == n - 1)
                        k += 1
                return mm

            def w(slot, a, b):
                return w_hi[:, slot, a:b], w_lo[:, slot, a:b]

            def u(kb):
                return blk(u_hi, kb), blk(u_lo, kb)

            def u_tokens(kb, t):
                a = kb * SEQ + t * P
                return u_hi[:, a:a + P], u_lo[:, a:a + P]

            def wide(a, b):
                return wide_hi[:, a:b], wide_lo[:, a:b]

            def token_sums(nn, b):
                pe.wait_ge(acc_ready, 9 * nn + 9)
                for t in range(TB):
                    mm = pe.matmul(bank[b][:, 2 * t:2 * t + 2], acc[:, t * P:(t + 1) * P], ones[:, 0:2],
                                   start=True, stop=True)
                mm.then_inc(tok_sum, 1)

            def row_sums(nn):
                pe.wait_ge(diag_ready, nn + 1)
                pe.matmul(bank[5][:, :], ones[:, :], diag[:, :], start=True, stop=True).then_inc(row_sum, 1)

            pe.wait_ge(ident_ready, 1)
            for m in range(KB):
                if m >= 4:
                    pe.wait_ge(h_ready, m - 3)
                for t in range(TB):
                    if m == 0:
                        pe.wait_ge(x_loaded[t], 16)
                    src = scratch if t < 3 else final_gb
                    a = (t * D if t < 3 else 0) + m * P
                    mm = pe.transpose(bank[4 + m % 4][:, t * P:(t + 1) * P], src[:, a:a + P], ident[:, :])
                mm.then_inc(x_turned, 1)

            def ffn(f, nn):
                base = FFN_BASE[f]

                def in_body(i):
                    peeled = type(i) is int
                    for r in range(IN_UNITS):
                        slot = (base + r) % SPLIT
                        pe.wait_ge(w_ready, base + 4 * i + r + 1)
                        if not peeled and r == 0:
                            pe.wait_ge(gate_scaled, FB * f + 2 * i)
                        if not peeled and r == 2:
                            pe.wait_ge(up_scaled, FB * f + 2 * i)
                        for q in range(4):
                            kb = 4 * (r % 2) + q
                            if peeled and r < 2:
                                pe.wait_ge(u_ready, 8 * nn + kb + 1)
                            for c in range(2):
                                a = q * 256 + c * P
                                mm = products(bank[2 * (r // 2) + c][:, :], [(w(slot, a, a + P), u(kb))],
                                              kb == 0, kb == KB - 1)
                        mm.then_inc(unit_used, 1)
                        if peeled and r == 1:
                            token_sums(nn, 5)
                        if peeled and r == 2:
                            row_sums(nn)

                in_body(0)
                with pe.Fori(1, IN_BODIES) as i:
                    in_body(i)
                pe.wait_ge(a_ready, FB * (f + 1) - 4)
                out_stage(base + IN_BODIES * IN_UNITS, nn + 1, OUT_KBS, 0, final_wait=FB * (f + 1))

            def out_stage(base, nn, kbs, at, final_wait=None):
                units = 2 * len(kbs)

                def body(i):
                    for r in range(units):
                        mp, k = divmod(r, len(kbs))
                        slot = (base + r) % SPLIT
                        pe.wait_ge(w_ready, base + units * i + r + 1)
                        if k == 0:
                            pe.wait_ge(h_ready, 8 * nn + 4 * i + 2 * mp - 2)
                        if final_wait is not None:
                            if r == len(kbs) - 2:
                                pe.wait_ge(a_ready, final_wait)
                        for q, kb in enumerate(kbs[k]):
                            for c in range(2):
                                a = q * 256 + c * P
                                mm = products(bank[4 + 2 * mp + c][:, :],
                                              [(w(slot, a, a + P), wide(at + kb * SEQ, at + (kb + 1) * SEQ))],
                                              kb == 0, kb == kbs[-1][-1])
                        mm.then_inc(unit_used, 1)

                with pe.Fori(0, OUT_BODIES) as i:
                    body(i)

            def mixer(m, nn):
                n = m.base
                if m.fox:
                    pe.wait_ge(w_ready, n + 1)
                    for kb in range(KB):
                        pe.wait_ge(u_ready, 8 * nn + kb + 1)
                        mm = products(bank[4][0:HEADS, :], [(w(n % SPLIT, kb * HEADS, (kb + 1) * HEADS), u(kb))],
                                      kb == 0, kb == KB - 1)
                    mm.then_inc(unit_used, 1)
                    n += 1
                    token_sums(nn, 5)
                    for k in range(V_UNITS):
                        pe.wait_ge(w_ready, n + 1)
                        if k == V_UNITS // 2:
                            pe.wait_ge(row_ready, nn + 1)
                            pe.wait_ge(f_chain, 1)
                        for t in range(TB):
                            for q in range(2):
                                kb = 2 * (k % 4) + q
                                mm = products(bank[4 * (k // 4) + t][:, :],
                                              [(u_tokens(kb, t), w(n % SPLIT, q * 512, (q + 1) * 512))],
                                              kb == 0, kb == KB - 1)
                        mm.then_inc(unit_used, 1)
                        n += 1
                        if k == 0:
                            row_sums(nn)
                else:
                    pe.wait_ge(w_ready, n + 1)
                    for kb in range(KB):
                        pe.wait_ge(u_ready, 8 * nn + kb + 1)
                        mm = products(bank[1][:, :], [(w(n % SPLIT, kb * P, (kb + 1) * P), u(kb))],
                                      kb == 0, kb == KB - 1)
                    mm.then_inc(unit_used, 1)
                    n += 1
                    token_sums(nn, 5)
                    pe.wait_ge(w_ready, n + 1)
                    for t in range(TB):
                        for kb in range(KB):
                            mm = products(bank[6][:, t * P:(t + 1) * P],
                                          [(u_tokens(kb, t), w(n % SPLIT, kb * P, (kb + 1) * P))],
                                          kb == 0, kb == KB - 1)
                    mm.then_inc(unit_used, 1)
                    n += 1
                    row_sums(nn)

                def project(n, b, free_at):
                    for kb in range(KB):
                        if kb == 0:
                            pe.wait_ge(w_ready, n + 1)
                            if free_at is not None:
                                pe.wait_ge(*free_at)
                        mm = products(bank[b][:, :], [(w(n % SPLIT, kb * P, (kb + 1) * P), u(kb))],
                                      kb == 0, kb == KB - 1)
                        if kb == KB - 1:
                            mm.then_inc(unit_used, 1)
                        yield

                def score(t, i):
                    par, j = t % 2, t // 2
                    q_at = (QB_AT if par else QA_AT) + (j % 2) * SEQ + i * P
                    k_at = K_AT + ((j if m.fox else t // (HEADS // KV_HEADS)) % 2) * SEQ + m.first_key[i] * P
                    nk = m.keys[i]
                    out = bank[m.bank[i]][:, m.bank_at[i]:m.bank_at[i] + nk]
                    products(out, [(wide(q_at, q_at + P), wide(k_at, k_at + nk))], True, False)
                    if m.fox:
                        pe.matmul(out, pick_r[:, t:t + 1].to_broadcast([P, P]), decay[:, 0:nk],
                                  start=False, stop=False)
                    before = 0 if m.fox or i == 0 else P
                    w_mask = before + P
                    pe.matmul(out[:, nk - w_mask:nk], ident_bf[:, :],
                              mask[:, m.n, 0 if before else 1:2, :].rearrange("p a k -> p (a k)"),
                              start=False, stop=True).then_inc(scored, 1)

                def turn(t, kb):
                    n_t = HEADS * m.n + t
                    at = TB * n_t + kb
                    if kb == 0:
                        pe.wait_ge(p_ready, n_t + 1)
                    if at >= 2:
                        pe.wait_ge(pt_ready, at - 1)
                    for k, i in enumerate(m.queries(kb)):
                        a = m.p_at[i] + (kb - m.first_key[i]) * P
                        mm = pe.transpose(bank[5 + at % 2][:, k * P:(k + 1) * P], prob[t % 2][:, a:a + P],
                                          ident[:, :])
                    mm.then_inc(turned, 1)

                def value(t, kb):
                    n_t = HEADS * m.n + t
                    at = TB * n_t + kb
                    pe.wait_ge(pt_ready, at + 1)
                    if kb == 0 and n_t:
                        pe.wait_ge(o_ready, n_t)
                    cols = P * len(m.queries(kb))
                    if m.fox:
                        v_at = V_AT + kb * D + t * DH
                    else:
                        v_at = V_AT + kb * P + t // (HEADS // KV_HEADS) * DH
                    p_at = PT_AT + (at % 2) * SEQ
                    k = 0
                    for a, b in ((0, 0), (0, 1), (1, 0)):
                        mm = pe.matmul(bank[7][0:DH, kb * P:kb * P + cols],
                                       (wide_hi, wide_lo)[a][:, v_at:v_at + DH],
                                       (wide_hi, wide_lo)[b][:, p_at:p_at + cols],
                                       start=kb == 0 and k == 0, stop=kb == TB - 1 and k == 2,
                                       skip_group_check=True)
                        k += 1
                    mm.then_inc(pv_done, 1)

                if m.fox:
                    for k, b in enumerate((0, 1)):
                        pe.wait_ge(v_ready, TB)
                        for _ in project(n, b, None):
                            pass
                        n += 1
                else:
                    for _ in project(n, 0, None):
                        pass
                    n += 1
                for t in range(HEADS + 1):
                    j = t // 2
                    fill = iter(())
                    if j + 1 < PAIRS and (m.fox or t % 2 == 0):
                        b = t % 2
                        done = 2 * j + 1 + b if m.fox else 2 * PAIRS + 2 + j
                        fill = project(n, b, (qk_scaled, done))
                        n += 1
                    steps = ["f", "f"]
                    if t < HEADS:
                        steps += [("s", 3), "f", ("s", 2), "f"]
                    if t:
                        steps += [("t", 0), "f"]
                    if t < HEADS:
                        steps += [("s", 0), ("s", 1)]
                    if t:
                        steps += [("t", 1), "f", ("v", 0), ("t", 2), "f", ("v", 1), ("t", 3), "f", ("v", 2)]
                    steps += ["f"] * (KB - steps.count("f"))
                    if t:
                        steps += [("v", 3)]
                    for s in steps:
                        if s == "f":
                            next(fill, None)
                        elif s[0] == "s":
                            if s[1] == 3:
                                if t == 0 and m.fox:
                                    pe.wait_ge(decay_ready, 1)
                                if t == 0:
                                    pe.wait_ge(v_ready, 2 * TB if m.fox else 3 * TB)
                                pe.wait_ge(qk_ready, m.qk_ready(j))
                            n_t = HEADS * m.n + t
                            if n_t:
                                pe.wait_ge(expd, TB * n_t)
                            score(t, s[1])
                        elif s[0] == "t":
                            turn(t - 1, s[1])
                        else:
                            value(t - 1, s[1])
                pe.wait_ge(o_ready, HEADS * (m.n + 1))
                out_stage(n, nn + 1, WO_KBS, O_AT)

            ffn(0, 0)
            mixer(Mixer(0), 1)
            ffn(1, 2)
            ffn(2, 3)
            mixer(Mixer(1), 4)
            ffn(3, 5)
            for half_d in range(2):
                for t in range(TB):
                    if half_d == 1 and t == TB - 1:
                        pe.wait_ge(ms_ready, 7)
                    for k in range(4):
                        m = 4 * half_d + k
                        if t == 0:
                            pe.wait_ge(h_ready, 8 * 6 + m + 1)
                        if t == 0 and half_d == 1 and k == 3:
                            token_sums(6, 7)
                        mm = pe.transpose(bank[4 * half_d + t][:, k * P:(k + 1) * P],
                                          h[:, m * SEQ + t * P:m * SEQ + (t + 1) * P], ident[:, :])
                    mm.then_inc(y_turned, 1)

        @block.scalar
        def _(act):
            act.dma_start(gain[:, :], gains).then_inc(small_loaded, 16)
            act.dma_start(bf[:, :], fox_b).then_inc(small_loaded, 16)
            act.dma_start(bq[:, :], swa_bq).then_inc(small_loaded, 16)
            act.dma_start(bk[:, :], swa_bk).then_inc(small_loaded, 16)
            act.dma_start(bv[:, :], swa_bv.to_broadcast([P, KV_HEADS * DH])).then_inc(small_loaded, 16)
            act.dma_start(sink[:, :], sinks.to_broadcast([P, HEADS])).then_inc(small_loaded, 16)

            def split_hi(n, r, base, cols, count=None):
                act.wait_ge(raw_loaded[(base + r) % RAW], count)
                slot = (base + r) % SPLIT
                act.activation(w_hi[:, slot, 0:cols], raw[:, (base + r) % RAW, 0:cols], ACT.Copy)\
                   .then_inc(w_hi_ready, 1)

            def split_next(used, base, r, turn_of, cols=UNIT):
                act.wait_ge(unit_used, used)
                q = r + LOOK
                split_hi(None, q, base, cols, 16 * (turn_of + (base + q) // RAW + 1))

            def post_block(nn, i4, r, first=False):
                m_at = (i4 + r) * SEQ
                if not first:
                    act.wait_ge(acc_ready, 9 * nn + i4 + r)
                act.wait_ge(h_ready, 8 * nn + i4 + r + 1)
                if nn < 6:
                    act.activation(dyn(u_hi, m_at), dyn(h, m_at), ACT.Copy,
                                   scale=gain[:, bass.ds(8 * nn + i4 + r, 1)]).then_inc(u_hi_ready, 1)
                act.activation(sq[:, r % 2, :], dyn(h, m_at), ACT.Square).then_inc(sq_ready, 1)

            act.wait_ge(small_loaded, 16 * 6)
            for n in range(LOOK):
                split_hi(n, n, 0, UNIT, 16)
            for m in range(KB):
                post_block(0, m - m % 2, m % 2, m == 0)
            act.wait_ge(x_turned, KB)
            act.dma_start(final_gb[:, :], final_g.to_broadcast([P, D])).then_inc(final_g_loaded, 16)

            def row_copy(nn):
                act.wait_ge(row_sum, nn + 1)
                act.activation(rstd_row[:, :], bank[5][:, :], ACT.Copy).then_inc(row_ready, 1)

            def ffn(f, nn, last):
                base = FFN_BASE[f]

                def in_body(i):
                    for r in range(IN_UNITS):
                        split_next(base + 4 * i + r + 1, base, r, i)
                        if type(i) is int and r == 2:
                            row_copy(nn)
                        if r == 2:
                            for c in range(2):
                                act.wait_ge(gate_scaled, FB * f + 2 * i + c + 1)
                                act.activation(silu_buf[:, c * SEQ:(c + 1) * SEQ],
                                               g_scaled_buf[:, c * SEQ:(c + 1) * SEQ], ACT.Silu)\
                                   .then_inc(silu_ready, 1)
                        if r == 3:
                            for c in range(2):
                                act.wait_ge(prod_ready, FB * f + 2 * i + c + 1)
                                act.activation(dyn(wide_hi, 2 * SEQ * i + c * SEQ),
                                               up_buf[:, c * SEQ:(c + 1) * SEQ], ACT.Copy)\
                                   .then_inc(a_hi_ready, 1)

                in_body(0)
                with act.Fori(1, IN_BODIES) as i:
                    in_body(i)
                out_stage(base + IN_BODIES * IN_UNITS, nn + 1, OUT_KBS, OUT_COLS, last)

            def out_stage(base, nn, kbs, cols, last=False):
                units = 2 * len(kbs)

                def body(i):
                    for r in range(units):
                        if not (last and type(i) is int and i == OUT_BODIES - 1 and r + LOOK >= units):
                            split_next(base + units * i + r + 1, base, r, units // RAW * i,
                                       cols if r + LOOK < units else UNIT)
                        if r % len(kbs) == len(kbs) - 1:
                            mp = r // len(kbs)
                            for c in range(2):
                                post_block(nn, 4 * i, 2 * mp + c)

                if last:
                    for i in range(OUT_BODIES):
                        body(i)
                else:
                    with act.Fori(0, OUT_BODIES) as i:
                        body(i)

            def mixer(m, nn):
                n = m.base

                def step(n):
                    split_next(n + 1, n, 0, 0)

                if m.fox:
                    step(n)
                    n += 1
                    step(n)
                    n += 1
                    row_copy(nn)
                    act.wait_ge(consts, 1)
                    act.wait_ge(f_chain, 3)
                    act.activation(scratch[0:HEADS, 512:1024], scratch[0:HEADS, 512:1024], ACT.Exp, scale=-1.0)\
                       .then_inc(f_act, 1)
                    act.wait_ge(f_act, 1)
                    act.activation(scratch[0:HEADS, 512:1024], scratch[0:HEADS, 512:1024], ACT.Ln,
                                   bias=ones[0:HEADS, 0:1]).then_inc(f_act, 1)
                    for k in range(1, V_UNITS):
                        step(n)
                        n += 1
                        if k == 1:
                            act.wait_ge(f_chain, 7)
                            act.activation(decay[0:HEADS, :], scratch[0:HEADS, 0:512], ACT.Copy)\
                               .then_inc(f_act, 1)
                        if k % 4 == 3:
                            for t in range(TB):
                                act.wait_ge(rstd_ready, nn + 1)
                                a = V_AT + t * D + (k // 4) * 512
                                act.activation(wide_hi[:, a:a + 512], bank[4 * (k // 4) + t][:, :], ACT.Copy,
                                               scale=rstd[:, t:t + 1]).then_inc(v_hi_ready, 1)
                else:
                    step(n)
                    n += 1
                    step(n)
                    n += 1
                    row_copy(nn)
                    for t in range(TB):
                        act.wait_ge(v_scaled, t + 1)
                        act.activation(wide_hi[:, V_AT + t * P:V_AT + (t + 1) * P], sq[:, 0, t * P:(t + 1) * P],
                                       ACT.Copy).then_inc(v_hi_ready, 1)
                    act.wait_ge(qk_scaled, 2 * PAIRS + 1)
                    for g in range(KV_HEADS):
                        for to in (g, 1 - g):
                            last = act.activation(
                                wide_hi[64 * to:64 * to + 64, K_AT + g * SEQ:K_AT + (g + 1) * SEQ],
                                scaled[64 * g:64 * g + 64, :], ACT.Copy)
                    last.then_inc(qk_hi_ready, 1)

                def project_hi(count, j, is_q):
                    act.wait_ge(qk_scaled, count)
                    if j >= 2:
                        act.wait_ge(scored, TB * (HEADS * m.n + 2 * (j - 1)))
                    if is_q:
                        a = (j % 2) * SEQ
                        act.wait_ge(zeroed, 4 * (m.n + 1))
                        act.activation(wide_hi[0:64, QA_AT + a:QA_AT + a + SEQ], scaled[0:64, :], ACT.Copy)
                        last = act.activation(wide_hi[64:128, QB_AT + a:QB_AT + a + SEQ], scaled[64:128, :],
                                              ACT.Copy)
                    else:
                        a = K_AT + (j % 2) * SEQ
                        last = act.activation(wide_hi[:, a:a + SEQ], scaled[:, :], ACT.Copy)
                    last.then_inc(qk_hi_ready, 1)

                count = 0 if m.fox else 2 * PAIRS + 1
                for k in range(2 if m.fox else 1):
                    step(n)
                    n += 1
                    count += 1
                    project_hi(count, 0, k == 0)

                for t in range(HEADS + 1):
                    j = t // 2
                    n_t = HEADS * m.n + t
                    b = n_t % 2

                    def pt_hi(kb):
                        at = TB * (n_t - 1) + kb
                        cols = P * len(m.queries(kb))
                        act.wait_ge(turned, at + 1)
                        if at >= 2:
                            act.wait_ge(pv_done, at - 1)
                        a = PT_AT + (at % 2) * SEQ
                        act.activation(wide_hi[:, a:a + cols], bank[5 + at % 2][:, 0:cols], ACT.Copy)\
                           .then_inc(pt_hi_ready, 1)

                    def exp(i):
                        nk = m.keys[i]
                        act.activation(prob[t % 2][:, m.p_at[i]:m.p_at[i] + nk],
                                       bank[m.bank[i]][:, m.bank_at[i]:m.bank_at[i] + nk], ACT.Exp,
                                       bias=nmax[:, b, i:i + 1], accum_out=psum_p[:, b, i:i + 1])\
                           .then_inc(expd, 1)

                    if t:
                        pt_hi(0)
                    if t < HEADS:
                        act.wait_ge(nmax_ready, n_t + 1)
                        if n_t >= 2:
                            act.wait_ge(turned, TB * (n_t - 1))
                            act.wait_ge(rsum_ready, n_t - 1)
                        exp(3)
                        exp(2)
                    if t:
                        pt_hi(1)
                    if t < HEADS:
                        exp(0)
                        exp(1)
                        if not m.fox:
                            act.activation(esink[:, b, :], nmax[:, b, :], ACT.Exp, bias=sink[:, t:t + 1])\
                               .then_inc(esink_ready, 1)
                    if t:
                        pt_hi(2)
                        pt_hi(3)
                    fill = j + 1 < PAIRS and (m.fox or t % 2 == 0)
                    if fill:
                        count += 1
                        project_hi(count, j + 1, t % 2 == 0)
                    if t:
                        par, jo = (t - 1) % 2, (t - 1) // 2
                        act.wait_ge(pv_done, TB * n_t)
                        act.activation(wide_hi[64 * par:64 * par + 64, O_AT + jo * SEQ:O_AT + (jo + 1) * SEQ],
                                       bank[7][0:DH, :], ACT.Copy).then_inc(o_hi_ready, 1)
                    if fill:
                        step(n)
                        n += 1
                out_stage(n, nn + 1, WO_KBS, UNIT)

            ffn(0, 0, False)
            mixer(Mixer(0), 1)
            ffn(1, 2, False)
            ffn(2, 3, False)
            mixer(Mixer(1), 4)
            ffn(3, 5, True)

        @block.vector
        def _(dve):
            def split_lo(n_mod, count, cols=UNIT):
                dve.wait_ge(w_hi_ready, count)
                s, r = n_mod % SPLIT, n_mod % RAW
                dve.tensor_tensor(w_lo[:, s, 0:cols], raw[:, r, 0:cols], f32(w_hi[:, s, 0:cols]),
                                  ALU.subtract).then_inc(w_ready, 1)

            def residual(nn, i4, r, src, scale):
                m_at = (i4 + r) * SEQ
                if scale is None:
                    dve.tensor_copy(dyn(h, m_at), src).then_inc(h_ready, 1)
                else:
                    dve.scalar_tensor_tensor(out=dyn(h, m_at), in0=src, scalar=scale, in1=dyn(h, m_at),
                                             op0=ALU.mult, op1=ALU.add).then_inc(h_ready, 1)

            def post_block(nn, i4, r):
                m_at = (i4 + r) * SEQ
                if nn < 6:
                    dve.wait_ge(u_hi_ready, 8 * nn + i4 + r + 1)
                    dve.scalar_tensor_tensor(out=dyn(u_lo, m_at), in0=dyn(h, m_at),
                                             scalar=gain[:, bass.ds(8 * nn + i4 + r, 1)],
                                             in1=f32(dyn(u_hi, m_at)), op0=ALU.mult, op1=ALU.subtract)\
                       .then_inc(u_ready, 1)
                dve.wait_ge(sq_ready, 8 * nn + i4 + r + 1)
                dve.wait_ge(acc_ready, 9 * nn + i4 + r + 1)
                dve.tensor_tensor(acc[:, :], acc[:, :], sq[:, r % 2, :], ALU.add).then_inc(acc_ready, 1)

            def mean_squares(nn, b):
                dve.wait_ge(tok_sum, nn + 1)
                dve.tensor_scalar(ms[:, :], bank[b][:, 0:2 * TB].rearrange("p (t two) -> p t two", two=2)[:, :, 0],
                                  1.0 / D, RMS_EPS, ALU.mult, ALU.add).then_inc(ms_ready, 1)
                if nn < 6:
                    dve.memset(acc[:, :], 0.0).then_inc(acc_ready, 1)

            def diagonals(nn):
                dve.wait_ge(rstd_ready, nn + 1)
                for t in range(TB):
                    last = dve.tensor_scalar(diag[:, t * P:(t + 1) * P], ident[:, :], rstd[:, t:t + 1], None,
                                             ALU.mult)
                last.then_inc(diag_ready, 1)

            dve.memset(acc[:, :], 0.0).then_inc(acc_ready, 1)
            dve.wait_ge(small_loaded, 16 * 6)
            dve.tensor_scalar(nsink[:, :], sink[:, :], -1.0, None, ALU.mult).then_inc(nsink_ready, 1)
            for n in range(LOOK):
                split_lo(n, n + 1)
            for m in range(KB):
                dve.wait_ge(x_turned, m + 1)
                residual(0, m, 0, bank[4 + m % 4][:, :], None)
            for m in range(KB):
                post_block(0, m - m % 2, m % 2)
            dve.wait_ge(consts, 1)
            dve.tensor_copy(pick_r[:, :], pick[:, :])

            def ffn(f, nn, last):
                base = FFN_BASE[f]

                def in_body(i):
                    first = type(i) is int
                    for r in range(IN_UNITS):
                        split_lo(base + r + LOOK, base + 4 * i + r + LOOK + 1)
                        if first and r == 1:
                            mean_squares(nn, 5)
                            diagonals(nn)
                        if r == (2 if first else 1):
                            dve.wait_ge(unit_used, base + 4 * i + 2)
                            if first:
                                dve.wait_ge(row_ready, nn + 1)
                            for c in range(2):
                                dve.tensor_tensor(g_scaled_buf[:, c * SEQ:(c + 1) * SEQ], bank[c][:, :],
                                                  rstd_row[:, :], ALU.mult).then_inc(gate_scaled, 1)
                        if r == 3:
                            dve.wait_ge(unit_used, base + 4 * i + 4)
                            for c in range(2):
                                dve.tensor_tensor(up_buf[:, c * SEQ:(c + 1) * SEQ], bank[2 + c][:, :],
                                                  rstd_row[:, :], ALU.mult).then_inc(up_scaled, 1)
                            for c in range(2):
                                up = up_buf[:, c * SEQ:(c + 1) * SEQ]
                                dve.wait_ge(silu_ready, FB * f + 2 * i + c + 1)
                                dve.wait_ge(up_scaled, FB * f + 2 * i + c + 1)
                                dve.tensor_tensor(up, up, silu_buf[:, c * SEQ:(c + 1) * SEQ], ALU.mult)\
                                   .then_inc(prod_ready, 1)
                            for c in range(2):
                                dve.wait_ge(a_hi_ready, FB * f + 2 * i + c + 1)
                                dve.tensor_tensor(dyn(wide_lo, 2 * SEQ * i + c * SEQ),
                                                  up_buf[:, c * SEQ:(c + 1) * SEQ],
                                                  f32(dyn(wide_hi, 2 * SEQ * i + c * SEQ)), ALU.subtract)\
                                   .then_inc(a_ready, 1)

                in_body(0)
                with dve.Fori(1, IN_BODIES) as i:
                    in_body(i)
                out_stage(base + IN_BODIES * IN_UNITS, nn + 1, OUT_KBS, 0.5, OUT_COLS, last)

            def out_stage(base, nn, kbs, scale, cols, last=False):
                units = 2 * len(kbs)

                def body(i):
                    for r in range(units):
                        if not (last and type(i) is int and i == OUT_BODIES - 1 and r + LOOK >= units):
                            split_lo(base + r + LOOK, base + units * i + r + LOOK + 1,
                                     cols if r + LOOK < units else UNIT)
                        if r % len(kbs) == len(kbs) - 1:
                            mp = r // len(kbs)
                            dve.wait_ge(unit_used, base + units * i + r + 1)
                            for c in range(2):
                                residual(nn, 4 * i, 2 * mp + c, bank[4 + 2 * mp + c][:, :], scale)
                            for c in range(2):
                                post_block(nn, 4 * i, 2 * mp + c)

                if last:
                    for i in range(OUT_BODIES):
                        body(i)
                else:
                    with dve.Fori(0, OUT_BODIES) as i:
                        body(i)

            def mixer(m, nn):
                n = m.base

                def step(n):
                    split_lo(n + LOOK, n + LOOK + 1)

                if m.fox:
                    x0, x1, x2, x3 = (scratch[0:HEADS, 512 * k:512 * k + 512] for k in range(4))
                    step(n)
                    n += 1
                    mean_squares(nn, 5)
                    diagonals(nn)
                    step(n)
                    n += 1
                    dve.wait_ge(row_ready, nn + 1)
                    dve.wait_ge(unit_used, m.base + 1)
                    dve.tensor_tensor(x0, bank[4][0:HEADS, :], rstd_row[0:HEADS, :], ALU.mult).then_inc(f_chain, 1)
                    dve.wait_ge(f_chain, 1)
                    dve.tensor_scalar(x0, x0, bf[:, 0:1], None, ALU.add).then_inc(f_chain, 1)
                    dve.wait_ge(f_chain, 2)
                    dve.scalar_tensor_tensor(out=x1, in0=x0, scalar=-1.0, in1=x0, op0=ALU.mult, op1=ALU.max)\
                       .then_inc(f_chain, 1)
                    dve.tensor_scalar(x3, x0, 0.0, None, ALU.min).then_inc(f_chain, 1)
                    for k in range(1, V_UNITS):
                        step(n)
                        if k == 1:
                            dve.wait_ge(f_act, 2)
                            dve.wait_ge(f_chain, 4)
                            dve.tensor_tensor(x2, x1, x3, ALU.subtract).then_inc(f_chain, 1)
                            dve.wait_ge(f_chain, 5)
                            dve.memset(x3, 1.0).then_inc(f_chain, 1)
                            dve.wait_ge(f_chain, 6)
                            dve.tensor_tensor_scan(x0, x3, x2, 0.0, ALU.mult, ALU.add).then_inc(f_chain, 1)
                        if k == 2:
                            dve.wait_ge(f_act, 3)
                            dve.tensor_tensor(decay[32:32 + HEADS, :], x0, f32(decay[0:HEADS, :]), ALU.subtract)\
                               .then_inc(decay_ready, 1)
                        n += 1
                        if k % 4 == 3:
                            for t in range(TB):
                                dve.wait_ge(v_hi_ready, TB * (k // 4) + t + 1)
                                a = V_AT + t * D + (k // 4) * 512
                                dve.scalar_tensor_tensor(out=wide_lo[:, a:a + 512], in0=bank[4 * (k // 4) + t][:, :],
                                                         scalar=rstd[:, t:t + 1], in1=f32(wide_hi[:, a:a + 512]),
                                                         op0=ALU.mult, op1=ALU.subtract).then_inc(v_ready, 1)
                else:
                    step(n)
                    n += 1
                    mean_squares(nn, 5)
                    diagonals(nn)
                    step(n)
                    n += 1
                    dve.wait_ge(unit_used, m.base + 2)
                    for t in range(TB):
                        dve.scalar_tensor_tensor(out=sq[:, 0, t * P:(t + 1) * P], in0=bank[6][:, t * P:(t + 1) * P],
                                                 scalar=rstd[:, t:t + 1], in1=bv[:, :], op0=ALU.mult, op1=ALU.add)\
                           .then_inc(v_scaled, 1)
                    dve.wait_ge(row_ready, nn + 1)
                    dve.wait_ge(qk_ready, 2 * PAIRS)
                    dve.tensor_tensor(scaled, bank[1][:, :], rstd_row[:, :], ALU.mult).then_inc(qk_raw, 1)
                    dve.wait_ge(qk_raw, 1)
                    dve.tensor_scalar(scaled, scaled, bk[:, 0:1], None, ALU.add).then_inc(qk_scaled, 1)
                    for t in range(TB):
                        dve.wait_ge(v_hi_ready, 2 * TB + t + 1)
                        a = V_AT + t * P
                        dve.tensor_tensor(wide_lo[:, a:a + P], sq[:, 0, t * P:(t + 1) * P], f32(wide_hi[:, a:a + P]),
                                          ALU.subtract).then_inc(v_ready, 1)
                    dve.wait_ge(qk_hi_ready, 2 * PAIRS + 1)
                    for g in range(KV_HEADS):
                        a = K_AT + g * SEQ
                        rows = slice(64 * g, 64 * g + 64)
                        for to in range(2):
                            last = dve.tensor_tensor(wide_lo[64 * to:64 * to + 64, a:a + SEQ], scaled[rows, :],
                                                     f32(wide_hi[rows, a:a + SEQ]), ALU.subtract)
                    last.then_inc(qk_ready, 1)

                def project_scaled(n, j, is_q, before):
                    if before:
                        dve.wait_ge(qk_ready, before)
                    dve.wait_ge(unit_used, n + 1)
                    src = bank[0 if is_q else 1][:, :]
                    if not m.fox:
                        dve.tensor_tensor(scaled, src, rstd_row[:, :], ALU.mult).then_inc(qk_raw, 1)
                        dve.wait_ge(qk_raw, 2 + j)
                        dve.tensor_scalar(scaled, scaled, bq[:, j:j + 1], QSCALE, ALU.add, ALU.mult)\
                           .then_inc(qk_scaled, 1)
                    elif is_q:
                        dve.scalar_tensor_tensor(out=scaled, in0=src, scalar=QSCALE, in1=rstd_row[:, :],
                                                 op0=ALU.mult, op1=ALU.mult).then_inc(qk_scaled, 1)
                    else:
                        dve.tensor_tensor(scaled, src, rstd_row[:, :], ALU.mult).then_inc(qk_scaled, 1)

                def project_lo(count, j, is_q):
                    dve.wait_ge(qk_hi_ready, count)
                    if is_q:
                        a = (j % 2) * SEQ
                        for at, rows in ((QA_AT + a, slice(0, 64)), (QB_AT + a, slice(64, 128))):
                            last = dve.tensor_tensor(wide_lo[rows, at:at + SEQ], scaled[rows, :],
                                                     f32(wide_hi[rows, at:at + SEQ]), ALU.subtract)
                    else:
                        a = K_AT + (j % 2) * SEQ
                        last = dve.tensor_tensor(wide_lo[:, a:a + SEQ], scaled, f32(wide_hi[:, a:a + SEQ]),
                                                 ALU.subtract)
                    last.then_inc(qk_ready, 1)

                count = 0 if m.fox else 2 * PAIRS + 1
                for k in range(2 if m.fox else 1):
                    step(n)
                    project_scaled(n, 0, k == 0, count)
                    n += 1
                    count += 1
                    project_lo(count, 0, k == 0)

                for t in range(HEADS + 1):
                    j = t // 2
                    n_t = HEADS * m.n + t
                    b = n_t % 2

                    def pt_lo(kb):
                        at = TB * (n_t - 1) + kb
                        cols = P * len(m.queries(kb))
                        a = PT_AT + (at % 2) * SEQ
                        dve.wait_ge(pt_hi_ready, at + 1)
                        dve.tensor_tensor(wide_lo[:, a:a + cols], bank[5 + at % 2][:, 0:cols],
                                          f32(wide_hi[:, a:a + cols]), ALU.subtract).then_inc(pt_ready, 1)

                    def row_max(i):
                        dve.wait_ge(scored, TB * n_t + (TB if i < 2 else ORDER.index(i) + 1))
                        return dve.tensor_reduce(nmax[:, b, i:i + 1],
                                                 bank[m.bank[i]][:, m.bank_at[i]:m.bank_at[i] + m.keys[i]],
                                                 AX_X, ALU.max, negate=True)

                    if t < HEADS:
                        if n_t >= 2:
                            dve.wait_ge(expd, TB * (n_t - 1))
                        row_max(3)
                        row_max(2)
                    if t:
                        pt_lo(0)
                    if t < HEADS:
                        row_max(0)
                        last = row_max(1)
                        if m.fox:
                            last.then_inc(nmax_ready, 1)
                        else:
                            last.then_inc(maxed, 1)
                            dve.wait_ge(maxed, t + 1)
                            dve.tensor_scalar(nmax[:, b, :], nmax[:, b, :], nsink[:, t:t + 1], None, ALU.min)\
                               .then_inc(nmax_ready, 1)
                    if t:
                        pt_lo(1)
                        pt_lo(2)
                        pt_lo(3)
                    fill = j + 1 < PAIRS and (m.fox or t % 2 == 0)
                    if fill:
                        project_scaled(n, j + 1, t % 2 == 0, count)
                    if t < HEADS:
                        dve.wait_ge(expd, TB * (n_t + 1))
                        if not m.fox:
                            dve.wait_ge(esink_ready, t + 1)
                            dve.tensor_tensor(psum_p[:, b, :], psum_p[:, b, :], esink[:, b, :], ALU.add)\
                               .then_inc(sum_ready, 1)
                            dve.wait_ge(sum_ready, t + 1)
                        dve.reciprocal(rsum[:, b, :], psum_p[:, b, :]).then_inc(rsum_ready, 1)
                        dve.wait_ge(rsum_ready, n_t + 1)
                        for i in ORDER:
                            part = prob[t % 2][:, m.p_at[i]:m.p_at[i] + m.keys[i]]
                            last = dve.tensor_scalar(part, part, rsum[:, b, i:i + 1], None, ALU.mult)
                        last.then_inc(p_ready, 1)
                    if fill:
                        count += 1
                        project_lo(count, j + 1, t % 2 == 0)
                    if t:
                        par, jo = (t - 1) % 2, (t - 1) // 2
                        rows = slice(64 * par, 64 * par + 64)
                        a = O_AT + jo * SEQ
                        dve.wait_ge(o_hi_ready, n_t)
                        dve.tensor_tensor(wide_lo[rows, a:a + SEQ], bank[7][0:DH, :], f32(wide_hi[rows, a:a + SEQ]),
                                          ALU.subtract).then_inc(o_ready, 1)
                    if fill:
                        step(n)
                        n += 1
                out_stage(n, nn + 1, WO_KBS, 1.0, UNIT)

            ffn(0, 0, False)
            mixer(Mixer(0), 1)
            ffn(1, 2, False)
            ffn(2, 3, False)
            mixer(Mixer(1), 4)
            ffn(3, 5, True)
            mean_squares(6, 7)
            dve.wait_ge(rstd_ready, 7)
            dve.wait_ge(final_g_loaded, 16)
            for n in range(2 * TB):
                t, half_d = n % TB, n // TB
                dve.wait_ge(y_turned, n + 1)
                dve.scalar_tensor_tensor(out=raw[:, n // 2, (n % 2) * 512:(n % 2 + 1) * 512], in0=bank[n][:, :],
                                         scalar=rstd[:, t:t + 1], in1=final_gb[:, half_d * 512:(half_d + 1) * 512],
                                         op0=ALU.mult, op1=ALU.mult).then_inc(y_scaled, 1)


def lay_out(inputs):
    a = {k: np.asarray(v) for k, v in inputs.items()}
    kb, pad = KB, np.zeros

    def columns(w, n):
        return w.reshape(kb, P, n, P).transpose(2, 1, 0, 3).reshape(n, P, UNIT)

    def wo(w):
        return w.reshape(2, 4, P, KB // 2, 256).transpose(3, 0, 2, 1, 4).reshape(WO_UNITS, P, UNIT)

    w_in = a["ffn_w_in"].reshape(4, 2, 4, P, 2, IN_BODIES, 256)
    ffn_in = w_in.transpose(0, 5, 4, 1, 3, 2, 6).reshape(4, IN_BODIES, IN_UNITS, P, UNIT)
    w_out = a["ffn_w_out"].reshape(4, FB, P, KB // 2, 256).transpose(0, 3, 2, 1, 4)
    ffn_out = pad((4, KB // 2, len(OUT_KBS), P, 3, 256), w_out.dtype)
    for u, kbs in enumerate(OUT_KBS):
        ffn_out[:, :, u, :, 0:len(kbs)] = w_out[:, :, :, kbs[0]:kbs[-1] + 1]
    ffn_out = ffn_out.reshape(4, KB // 2 * len(OUT_KBS) // RAW, RAW, P, OUT_COLS)

    fox = a["fox_w_in"][0]
    w_f = pad((1, P, UNIT), fox.dtype)
    w_f[0, :, 0:kb * HEADS] = fox[:, 3 * D:].reshape(kb, P, HEADS).transpose(1, 0, 2).reshape(P, kb * HEADS)
    w_v = fox[:, 2 * D:3 * D].reshape(4, 2, P, 2, 512).transpose(3, 0, 2, 1, 4).reshape(V_UNITS, P, UNIT)
    qk = np.stack([columns(fox[:, 0:D], PAIRS), columns(fox[:, D:2 * D], PAIRS)], 1).reshape(2 * PAIRS, P, UNIT)
    swa = a["swa_w_in"][0]
    kv = columns(swa[:, D:D + 2 * P], 2)
    mix_w = np.concatenate([w_f, w_v, qk, wo(a["fox_w_o"][0]), kv, columns(swa[:, 0:D], PAIRS), wo(a["swa_w_o"][0])])
    b = a["swa_b_in"][0]
    return {
        "x": a["x"].reshape(SEQ, D),
        "gains": a["norm_g"].reshape(6, KB, P).transpose(2, 0, 1).reshape(P, 6 * KB),
        "final_g": a["final_g"].reshape(1, D),
        "ffn_in": ffn_in,
        "ffn_out": ffn_out,
        "mix_w": mix_w,
        "fox_b": a["fox_b_f"].reshape(HEADS, 1),
        "swa_bq": b[0:D].reshape(PAIRS, P).transpose(1, 0),
        "swa_bk": b[D:D + P].reshape(P, 1),
        "swa_bv": b[D + P:D + 2 * P].reshape(1, P),
        "sinks": a["swa_sinks"].reshape(1, HEADS),
    }


def kernel(**inputs):
    import concourse.bacc as bacc
    from concourse.bass_utils import run_bass_kernel_spmd

    nc = bacc.Bacc("TRN2", target_bir_lowering=False, num_devices=1)
    arrays = {k: np.ascontiguousarray(v) for k, v in lay_out(inputs).items()}
    args = {k: nc.dram_tensor(k + "_dram", v.shape, mybir.dt.from_np(v.dtype), kind="ExternalInput").ap()
            for k, v in arrays.items()}
    y = nc.dram_tensor("y_dram", (SEQ, D), F32, kind="ExternalOutput").ap()
    build(nc, y=y, **args)
    r = run_bass_kernel_spmd(nc, [{k + "_dram": v for k, v in arrays.items()}], core_ids=[0])
    return r.results[0]["y_dram"].reshape(1, SEQ, D)
```

```python
from contextlib import ExitStack

import numpy as np

import concourse.bass as bass
from concourse import mybir

F32 = mybir.dt.float32
F32R = mybir.dt.float32r
BF16 = mybir.dt.bfloat16
ALU = mybir.AluOpType
ACT = mybir.ActivationFunctionType
AX_X = mybir.AxisListType.X

P = 128
SEQ = 512
D = 1024
DFF = 2816
HEADS = 16
DH = 64
KV_HEADS = 2
TB = SEQ // P
KB = D // P
FB = DFF // P
PAIRS = HEADS // 2
RMS_EPS = 1e-6
QSCALE = DH ** -0.5
MASKED = -1e30

RAW = 4
SPLIT = 2
UNIT = 1024
LOOK = SPLIT

IN_BODIES = FB // 2
IN_UNITS = 4
OUT_KBS = [range(3 * u, 3 * u + 3) for u in range(6)] + [range(18, 20), range(20, 22)]
OUT_COLS = 3 * 256
OUT_BODIES = 2
WO_KBS = [range(0, 4), range(4, 8)]

FFN_UNITS = IN_BODIES * IN_UNITS + (KB // 2) * len(OUT_KBS)
WO_UNITS = (KB // 2) * len(WO_KBS)
V_UNITS = 8
FOX_UNITS = 1 + V_UNITS + 2 * PAIRS + WO_UNITS
SWA_UNITS = 2 + PAIRS + WO_UNITS
FFN_BASE = [0, FFN_UNITS + FOX_UNITS, 2 * FFN_UNITS + FOX_UNITS, 3 * FFN_UNITS + FOX_UNITS + SWA_UNITS]
MIX_BASE = [FFN_UNITS, 3 * FFN_UNITS + FOX_UNITS]
TOTAL_UNITS = 4 * FFN_UNITS + FOX_UNITS + SWA_UNITS


FOX_BASE, SWA_BASE = MIX_BASE

FOX_KEYS = [(i + 1) * P for i in range(TB)]
FOX_BANK = [2, 2, 3, 4]
FOX_BANK_AT = [0, P, 0, 0]
FOX_P_AT = [sum(FOX_KEYS[:i]) for i in range(TB)]

CHUNK = 64
CHUNKS = SEQ // CHUNK
HALF = CHUNKS // 2
GROUP_PAIRS = PAIRS // KV_HEADS

ORDER = (3, 2, 0, 1)


def build(nc, x, gains, final_g, ffn_in, ffn_out, mix_w, fox_b, swa_bq, swa_bk, swa_bv, sinks, y):
    ctx = ExitStack()
    with ctx:
        def sb(name, shape, dt=F32):
            return ctx.enter_context(nc.sbuf_tensor(name, shape, dt))

        def sem(name):
            return ctx.enter_context(nc.semaphore(name))

        h = sb("h", [P, KB * SEQ])
        u_hi = sb("u_hi", [P, KB * SEQ], F32R)
        u_lo = sb("u_lo", [P, KB * SEQ], F32R)
        wide_hi = sb("wide_hi", [P, 12288], F32R)
        wide_lo = sb("wide_lo", [P, 12288], F32R)
        V_AT, O_AT, PT_AT, K_AT, QA_AT, QB_AT = 0, 4096, 8192, 9216, 10240, 11264
        raw = sb("raw", [P, RAW, UNIT])
        w_hi = sb("w_hi", [P, SPLIT, UNIT], F32R)
        w_lo = sb("w_lo", [P, SPLIT, UNIT], F32R)
        scratch = sb("scratch", [P, 6 * SEQ])
        final_gb = sb("final_gb", [P, D])
        rstd_row = sb("rstd_row", [P, SEQ])
        sq = sb("sq", [P, 2, SEQ])
        acc = sb("acc", [P, SEQ])
        diag = sb("diag", [P, SEQ])
        gain = sb("gain", [P, 6 * KB])
        ident = sb("ident", [P, P])
        ones = sb("ones", [P, P])
        ident_bf = sb("ident_bf", [P, P], BF16)
        causal = sb("causal", [P, P], BF16)
        all_masked = sb("all_masked", [P, CHUNK], BF16)
        ms = sb("ms", [P, TB])
        half = sb("half", [P, TB])
        rstd = sb("rstd", [P, TB])
        bf = sb("bf", [HEADS, 1])
        bq = sb("bq", [P, PAIRS])
        bq_scaled = sb("bq_scaled", [P, PAIRS])
        bk = sb("bk", [P, 1])
        bv = sb("bv", [P, 1])
        sink = sb("sink", [P, PAIRS])
        nsink = sb("nsink", [P, PAIRS])
        nmax = sb("nmax", [P, 2, TB])
        psum_p = sb("psum_p", [P, 2, TB])
        wmax = sb("wmax", [P, 2, CHUNKS])
        wsum = sb("wsum", [P, 2, CHUNKS])
        wrsum = sb("wrsum", [P, 2, CHUNKS])
        esink = sb("esink", [P, 2, CHUNKS])
        rsum = sb("rsum", [P, 2, TB])
        pick = sb("pick", [P, HEADS])
        pick_r = sb("pick_r", [P, HEADS], F32R)
        decay = sb("decay", [P, SEQ], F32R)
        g_scaled_buf, silu_buf, up_buf = (scratch[:, 2 * n * SEQ:2 * (n + 1) * SEQ] for n in range(3))
        prob = [scratch[:, 0:1280], scratch[:, 1280:2560]]
        scaled = scratch[:, 2560:3072]
        wprob = [scratch[:, 0:CHUNKS * P], scratch[:, CHUNKS * P:2 * CHUNKS * P]]
        bank = [ctx.enter_context(nc.psum_tensor(f"bank{b}", [P, 512], F32)) for b in range(8)]

        x_loaded = [sem(f"x_loaded{t}") for t in range(TB)]
        small_loaded = sem("small_loaded")
        final_g_loaded = sem("final_g_loaded")
        raw_loaded = [sem(f"raw_loaded{s}") for s in range(RAW)]
        w_hi_ready = sem("w_hi_ready")
        w_ready = sem("w_ready")
        unit_used = sem("unit_used")
        consts = sem("consts")
        consts_pool = sem("consts_pool")
        ident_ready = sem("ident_ready")
        x_turned = sem("x_turned")
        h_ready = sem("h_ready")
        u_hi_ready = sem("u_hi_ready")
        u_ready = sem("u_ready")
        sq_ready = sem("sq_ready")
        acc_ready = sem("acc_ready")
        tok_sum = sem("tok_sum")
        ms_ready = sem("ms_ready")
        rstd_ready = sem("rstd_ready")
        diag_ready = sem("diag_ready")
        row_sum = sem("row_sum")
        row_ready = sem("row_ready")
        gate_scaled = sem("gate_scaled")
        silu_ready = sem("silu_ready")
        up_scaled = sem("up_scaled")
        prod_ready = sem("prod_ready")
        a_hi_ready = sem("a_hi_ready")
        a_ready = sem("a_ready")
        f_chain = sem("f_chain")
        f_act = sem("f_act")
        decay_ready = sem("decay_ready")
        v_hi_ready = sem("v_hi_ready")
        v_ready = sem("v_ready")
        zeroed = sem("zeroed")
        qk_scaled = sem("qk_scaled")
        qk_hi_ready = sem("qk_hi_ready")
        qk_ready = sem("qk_ready")
        scored = sem("scored")
        nmax_ready = sem("nmax_ready")
        biases_ready = sem("biases_ready")
        expd = sem("expd")
        rsum_ready = sem("rsum_ready")
        p_ready = sem("p_ready")
        turned = sem("turned")
        pt_hi_ready = sem("pt_hi_ready")
        pt_ready = sem("pt_ready")
        pv_done = sem("pv_done")
        o_hi_ready = sem("o_hi_ready")
        o_ready = sem("o_ready")
        w_v_scaled = sem("w_v_scaled")
        w_v_biased = sem("w_v_biased")
        w_v_turned = sem("w_v_turned")
        w_v_hi_ready = sem("w_v_hi_ready")
        w_v_ready = sem("w_v_ready")
        v_moved_hi = sem("v_moved_hi")
        v_moved = sem("v_moved")
        w_k_scaled = sem("w_k_scaled")
        w_k_hi_ready = sem("w_k_hi_ready")
        w_k_ready = sem("w_k_ready")
        w_q_scaled = sem("w_q_scaled")
        w_q_hi_ready = sem("w_q_hi_ready")
        w_q_ready = sem("w_q_ready")
        w_scored = sem("w_scored")
        w_maxed = sem("w_maxed")
        w_nmax_ready = sem("w_nmax_ready")
        w_expd = sem("w_expd")
        w_esink_ready = sem("w_esink_ready")
        w_sum_ready = sem("w_sum_ready")
        w_rsum_ready = sem("w_rsum_ready")
        w_p_ready = sem("w_p_ready")
        w_turned = sem("w_turned")
        w_pt_hi_ready = sem("w_pt_hi_ready")
        w_pt_ready = sem("w_pt_ready")
        w_pv_done = sem("w_pv_done")
        w_o_hi_ready = sem("w_o_hi_ready")
        w_o_ready = sem("w_o_ready")
        y_turned = sem("y_turned")
        y_scaled = sem("y_scaled")
        y_stored = sem("y_stored")

        def window_q(part, par, first=0, count=2 * CHUNKS):
            a = QA_AT + first * P
            rows = part[64 * par:64 * par + 64, a:a + count * P]
            return rows.rearrange("p (n par q) -> p n par q", par=2, q=CHUNK)[:, :, par, :]

        def window_q_zero(part, par):
            rows = part[64 - 64 * par:128 - 64 * par, QA_AT:QA_AT + 2 * CHUNKS * P]
            return rows.rearrange("p (n par q) -> p n par q", par=2, q=CHUNK)[:, :, par, :]

        def pair_output(b, par):
            return b[0:DH, :].rearrange("p (n par q) -> p n par q", par=2, q=CHUNK)[:, :, par, :]

        def chunks(ap):
            return ap.rearrange("p (n c) -> p n c", c=CHUNK)

        VS_AT = V_AT + SEQ

        block = ctx.enter_context(nc.Block())

        def blk(t, m, n=1):
            return t[:, m * SEQ:(m + n) * SEQ]

        def f32(ap):
            return ap.bitcast(F32)

        def dyn(t, start, size=SEQ):
            return t[:, bass.ds(start, size)]

        @block.sync
        def _(sp):
            x_at = [scratch[:, 0:D], scratch[:, D:2 * D], scratch[:, 2 * D:3 * D], final_gb[:, :]]
            for t in range(TB):
                sp.dma_start(x_at[t], x[t * P:(t + 1) * P, :]).then_inc(x_loaded[t], 16)

            def load(n, slot, src, cols, wait=None):
                if wait is not None:
                    sp.wait_ge(w_ready, wait)
                sp.dma_start(raw[:, slot, 0:cols], src).then_inc(raw_loaded[slot], 16)

            def load_ffn(f):
                base = FFN_BASE[f]

                def load_in(i):
                    for r in range(IN_UNITS):
                        load(r, (base + r) % RAW, ffn_in[f, i, r], UNIT,
                             None if f == 0 and type(i) is int and i == 0 else base + 4 * i + r - RAW + 1)

                load_in(0)
                with sp.Fori(1, IN_BODIES) as i:
                    load_in(i)
                out = base + IN_BODIES * IN_UNITS
                with sp.Fori(0, (KB // 2) * len(OUT_KBS) // RAW) as i:
                    for r in range(RAW):
                        load(r, (out + r) % RAW, ffn_out[f, i, r], OUT_COLS, out + 4 * i + r - RAW + 1)

            def load_mixer(base, first, units):
                for n in range(units):
                    load(n, (base + n) % RAW, mix_w[first + n], UNIT, base + n - RAW + 1)

            load_ffn(0)
            load_mixer(FOX_BASE, 0, FOX_UNITS)
            load_ffn(1)
            load_ffn(2)
            load_mixer(SWA_BASE, FOX_UNITS, SWA_UNITS)
            load_ffn(3)
            for n in range(2 * TB):
                t, half_d = n % TB, n // TB
                sp.wait_ge(y_scaled, n + 1)
                sp.dma_start(y[t * P:(t + 1) * P, half_d * 512:(half_d + 1) * 512],
                             raw[:, n // 2, (n % 2) * 512:(n % 2 + 1) * 512]).then_inc(y_stored, 16)
            sp.wait_ge(y_stored, 16 * 2 * TB)

        @block.gpsimd
        def _(pool):
            def in_turn(k, ins, s):
                ins.then_inc(s, 1)
                pool.wait_ge(s, k)

            in_turn(1, pool.memset(ones[:, :], 1.0), consts_pool)
            in_turn(2, pool.memset(ident[:, :], 0.0), consts_pool)
            in_turn(3, pool.affine_select(out=ident[:, :], in_=ident[:, :], compare_op=ALU.not_equal, fill=1.0,
                                          base=0, pattern=[[-1, P]], channel_multiplier=1), consts_pool)
            pool.memset(half[:, :], -0.5).then_inc(ident_ready, 1)
            in_turn(4, pool.memset(ident_bf[:, :], 0.0), consts_pool)
            in_turn(5, pool.affine_select(out=ident_bf[:, :], in_=ident_bf[:, :], compare_op=ALU.not_equal,
                                          fill=1.0, base=0, pattern=[[-1, P]], channel_multiplier=1), consts_pool)
            in_turn(6, pool.memset(causal[:, :], 0.0), consts_pool)
            in_turn(7, pool.affine_select(out=causal[:, :], in_=causal[:, :], compare_op=ALU.is_ge, fill=MASKED,
                                          base=0, pattern=[[-1, P]], channel_multiplier=1), consts_pool)
            in_turn(8, pool.memset(all_masked[:, :], MASKED), consts_pool)
            in_turn(9, pool.memset(f32(decay[:, :]), 0.0), consts_pool)
            in_turn(10, pool.memset(pick[:, :], 0.0), consts_pool)
            in_turn(11, pool.affine_select(out=pick[:, :], in_=pick[:, :], compare_op=ALU.not_equal, fill=1.0,
                                           base=0, pattern=[[-1, HEADS]], channel_multiplier=1), consts_pool)
            pool.affine_select(out=pick[:, :], in_=pick[:, :], compare_op=ALU.not_equal, fill=1.0,
                               base=-32, pattern=[[-1, HEADS]], channel_multiplier=1).then_inc(consts, 1)
            pool.wait_ge(consts, 1)

            def pow_rstd(nn):
                pool.wait_ge(ms_ready, nn + 1)
                pool.tensor_tensor(rstd[:, :], ms[:, :], half[:, :], ALU.pow).then_inc(rstd_ready, 1)

            def zero_fox_halves():
                pool.wait_ge(unit_used, FOX_BASE)
                for k, part in enumerate((wide_hi, wide_lo)):
                    in_turn(2 * k + 1, pool.memset(f32(part[64:128, QA_AT:QA_AT + 2 * SEQ]), 0.0), zeroed)
                    in_turn(2 * k + 2, pool.memset(f32(part[0:64, QB_AT:QB_AT + 2 * SEQ]), 0.0), zeroed)

            def zero_window_halves():
                pool.wait_ge(unit_used, SWA_BASE)
                for k, part in enumerate((wide_hi, wide_lo)):
                    for par in range(2):
                        in_turn(4 + 2 * k + par + 1, pool.memset(f32(window_q_zero(part, par)), 0.0), zeroed)

            pow_rstd(0)
            zero_fox_halves()
            pow_rstd(1)
            pow_rstd(2)
            pow_rstd(3)
            zero_window_halves()
            pow_rstd(4)
            pow_rstd(5)
            pow_rstd(6)

        @block.tensor
        def _(pe):
            def products(out, pairs, first, last):
                n = 3 * len(pairs)
                k = 0
                for (a_hi, a_lo), (b_hi, b_lo) in pairs:
                    for a, b in ((a_hi, b_hi), (a_hi, b_lo), (a_lo, b_hi)):
                        mm = pe.matmul(out, a, b, start=first and k == 0, stop=last and k == n - 1)
                        k += 1
                return mm

            def w(slot, a, b):
                return w_hi[:, slot, a:b], w_lo[:, slot, a:b]

            def u(kb):
                return blk(u_hi, kb), blk(u_lo, kb)

            def u_tokens(kb, t):
                a = kb * SEQ + t * P
                return u_hi[:, a:a + P], u_lo[:, a:a + P]

            def wide(a, b):
                return wide_hi[:, a:b], wide_lo[:, a:b]

            def token_sums(nn, b):
                pe.wait_ge(acc_ready, 9 * nn + 9)
                for t in range(TB):
                    mm = pe.matmul(bank[b][:, 2 * t:2 * t + 2], acc[:, t * P:(t + 1) * P], ones[:, 0:2],
                                   start=True, stop=True)
                mm.then_inc(tok_sum, 1)

            def row_sums(nn):
                pe.wait_ge(diag_ready, nn + 1)
                pe.matmul(bank[5][:, :], ones[:, :], diag[:, :], start=True, stop=True).then_inc(row_sum, 1)

            pe.wait_ge(ident_ready, 1)
            for m in range(KB):
                if m >= 4:
                    pe.wait_ge(h_ready, m - 3)
                for t in range(TB):
                    if m == 0:
                        pe.wait_ge(x_loaded[t], 16)
                    src = scratch if t < 3 else final_gb
                    a = (t * D if t < 3 else 0) + m * P
                    mm = pe.transpose(bank[4 + m % 4][:, t * P:(t + 1) * P], src[:, a:a + P], ident[:, :])
                mm.then_inc(x_turned, 1)

            def ffn(f, nn):
                base = FFN_BASE[f]

                def in_body(i):
                    peeled = type(i) is int
                    for r in range(IN_UNITS):
                        slot = (base + r) % SPLIT
                        pe.wait_ge(w_ready, base + 4 * i + r + 1)
                        if not peeled and r == 0:
                            pe.wait_ge(gate_scaled, FB * f + 2 * i)
                        if not peeled and r == 2:
                            pe.wait_ge(up_scaled, FB * f + 2 * i)
                        for q in range(4):
                            kb = 4 * (r % 2) + q
                            if peeled and r < 2:
                                pe.wait_ge(u_ready, 8 * nn + kb + 1)
                            for c in range(2):
                                a = q * 256 + c * P
                                mm = products(bank[2 * (r // 2) + c][:, :], [(w(slot, a, a + P), u(kb))],
                                              kb == 0, kb == KB - 1)
                        mm.then_inc(unit_used, 1)
                        if peeled and r == 1:
                            token_sums(nn, 5)
                        if peeled and r == 2:
                            row_sums(nn)

                in_body(0)
                with pe.Fori(1, IN_BODIES) as i:
                    in_body(i)
                pe.wait_ge(a_ready, FB * (f + 1) - 4)
                out_stage(base + IN_BODIES * IN_UNITS, nn + 1, OUT_KBS, 0, final_wait=FB * (f + 1))

            def out_pair(n, free, free_count, ready, per_pair):
                for k, kbs in enumerate(WO_KBS):
                    for q, kb in enumerate(kbs):
                        if kb == 0:
                            pe.wait_ge(free, free_count)
                        if q == 0:
                            pe.wait_ge(w_ready, n + k + 1)
                        pe.wait_ge(ready, per_pair * (kb + 1))
                        for c in range(2):
                            a = q * 256 + c * P
                            o_at = O_AT + kb * SEQ
                            mm = products(bank[c][:, :], [(w((n + k) % SPLIT, a, a + P), wide(o_at, o_at + SEQ))],
                                          kb == 0, kb == KB - 1)
                        if q == len(kbs) - 1:
                            mm.then_inc(unit_used, 1)
                        yield

            def out_stage(base, nn, kbs, at, final_wait=None, first_done=False):
                units = 2 * len(kbs)

                def body(i, start=0):
                    for r in range(start, units):
                        mp, k = divmod(r, len(kbs))
                        slot = (base + r) % SPLIT
                        pe.wait_ge(w_ready, base + units * i + r + 1)
                        if k == 0:
                            pe.wait_ge(h_ready, 8 * nn + 4 * i + 2 * mp - 2 * (1 + (start > 0)))
                        if final_wait is not None:
                            if r == len(kbs) - 2:
                                pe.wait_ge(a_ready, final_wait)
                        for q, kb in enumerate(kbs[k]):
                            for c in range(2):
                                a = q * 256 + c * P
                                mm = products(bank[4 + 2 * mp + c][:, :],
                                              [(w(slot, a, a + P), wide(at + kb * SEQ, at + (kb + 1) * SEQ))],
                                              kb == 0, kb == kbs[-1][-1])
                        mm.then_inc(unit_used, 1)

                if first_done:
                    body(0, len(kbs))
                    body(1)
                else:
                    with pe.Fori(0, OUT_BODIES) as i:
                        body(i)

            def project(n, b, free_at):
                for kb in range(KB):
                    if kb == 0:
                        pe.wait_ge(w_ready, n + 1)
                        if free_at is not None:
                            pe.wait_ge(*free_at)
                    mm = products(bank[b][:, :], [(w(n % SPLIT, kb * P, (kb + 1) * P), u(kb))],
                                  kb == 0, kb == KB - 1)
                    if kb == KB - 1:
                        mm.then_inc(unit_used, 1)
                    yield

            def fox(nn):
                n = FOX_BASE
                for k in range(V_UNITS):
                    pe.wait_ge(w_ready, n + 1)
                    if k == 0:
                        pe.wait_ge(u_ready, 8 * nn + 2)
                    if k == V_UNITS // 2:
                        pe.wait_ge(row_ready, nn + 1)
                        pe.wait_ge(f_chain, 1)
                    for t in range(TB):
                        for q in range(2):
                            kb = 2 * (k % 4) + q
                            mm = products(bank[4 * (k // 4) + t][:, :],
                                          [(u_tokens(kb, t), w(n % SPLIT, q * 512, (q + 1) * 512))],
                                          kb == 0, kb == KB - 1)
                    mm.then_inc(unit_used, 1)
                    n += 1
                    if k == 0:
                        pe.wait_ge(w_ready, n + 1)
                        for kb in range(KB):
                            pe.wait_ge(u_ready, 8 * nn + kb + 1)
                            mm = products(bank[4][0:HEADS, :], [(w(n % SPLIT, kb * HEADS, (kb + 1) * HEADS), u(kb))],
                                          kb == 0, kb == KB - 1)
                        mm.then_inc(unit_used, 1)
                        n += 1
                        token_sums(nn, 5)
                    if k == 1:
                        row_sums(nn)

                def score(t, i):
                    par, j = t % 2, t // 2
                    q_at = (QB_AT if par else QA_AT) + (j % 2) * SEQ + i * P
                    k_at = K_AT + (j % 2) * SEQ
                    nk = FOX_KEYS[i]
                    out = bank[FOX_BANK[i]][:, FOX_BANK_AT[i]:FOX_BANK_AT[i] + nk]
                    products(out, [(wide(q_at, q_at + P), wide(k_at, k_at + nk))], True, False)
                    pe.matmul(out, pick_r[:, t:t + 1].to_broadcast([P, P]), decay[:, 0:nk],
                              start=False, stop=False)
                    pe.matmul(out[:, nk - P:nk], ident_bf[:, :], causal[:, :],
                              start=False, stop=True).then_inc(scored, 1)

                def turn(t, kb):
                    at = TB * t + kb
                    if kb == 0:
                        pe.wait_ge(p_ready, t + 1)
                    if at >= 2:
                        pe.wait_ge(pt_ready, at - 1)
                    for k, i in enumerate(range(kb, TB)):
                        a = FOX_P_AT[i] + kb * P
                        mm = pe.transpose(bank[5 + at % 2][:, k * P:(k + 1) * P], prob[t % 2][:, a:a + P],
                                          ident[:, :])
                    mm.then_inc(turned, 1)

                def value(t, kb):
                    at = TB * t + kb
                    pe.wait_ge(pt_ready, at + 1)
                    if kb == 0 and t:
                        pe.wait_ge(o_ready, t)
                    v_at = V_AT + kb * D + t * DH
                    p_at = PT_AT + (at % 2) * SEQ
                    cols = SEQ - kb * P
                    products(bank[7][0:DH, kb * P:SEQ],
                             [(wide(v_at, v_at + DH), wide(p_at, p_at + cols))], kb == 0, kb == TB - 1)\
                        .then_inc(pv_done, 1)

                def fillers(n):
                    for m in range(2 * PAIRS):
                        yield from project(n + m, m % 2, (qk_scaled, m - 1) if m >= 2 else None)
                    yield from out_pair(n + 2 * PAIRS, qk_scaled, 2 * PAIRS, o_ready, 2)

                fill = fillers(n)
                n += 2 * PAIRS + len(WO_KBS)
                AHEAD = 3
                pe.wait_ge(v_ready, TB)
                for _ in range(2 * KB + AHEAD):
                    next(fill)
                for t in range(HEADS + 1):
                    j = t // 2
                    steps = ["f", "f"]
                    if t < HEADS:
                        steps += [("s", 3), "f", ("s", 2), "f"]
                    if t:
                        steps += [("t", 0), "f"]
                    if t < HEADS:
                        steps += [("s", 0), ("s", 1)]
                    if t:
                        steps += [("t", 1), "f", ("v", 0), ("t", 2), "f", ("v", 1), ("t", 3), "f", ("v", 2)]
                    steps += ["f"] * (KB - steps.count("f"))
                    if t:
                        steps += [("v", 3)]
                    allowed = {HEADS - 3: range(KB - AHEAD), HEADS - 2: (0, 3, 6), HEADS - 1: (0, 5),
                               HEADS: (0, 1)}.get(t, range(KB))
                    fillers = 0
                    for s in steps:
                        if s == "f":
                            if fillers in allowed:
                                next(fill, None)
                            fillers += 1
                        elif s[0] == "s":
                            if s[1] == 3:
                                if t == 0:
                                    pe.wait_ge(decay_ready, 1)
                                    pe.wait_ge(v_ready, 2 * TB)
                                pe.wait_ge(qk_ready, 2 * j + 2)
                            if t:
                                pe.wait_ge(expd, TB * t)
                            score(t, s[1])
                        elif s[0] == "t":
                            turn(t - 1, s[1])
                        else:
                            value(t - 1, s[1])
                for _ in fill:
                    pass
                out_stage(n - len(WO_KBS), nn + 1, WO_KBS, O_AT, first_done=True)

            def window(nn):
                n = SWA_BASE
                k_steps, v_steps = project(n, 1, None), project(n + 1, 2, None)
                n += 2
                for steps, first, last in ((k_steps, 0, 6), (v_steps, 0, 6), (k_steps, 6, 8), (v_steps, 6, 8)):
                    for kb in range(first, last):
                        pe.wait_ge(u_ready, 8 * nn + kb + 1)
                        if kb < KB - 1:
                            next(steps)
                        else:
                            for _ in steps:
                                pass
                token_sums(nn, 5)

                def score(j, half):
                    if j:
                        pe.wait_ge(w_expd, CHUNKS * (j - 1) + HALF * (half + 1))
                    for n in range(HALF * half, HALF * (half + 1)):
                        out = bank[2 + half][:, (n % HALF) * P:(n % HALF + 1) * P]
                        k_at = K_AT + j // GROUP_PAIRS * SEQ + max(0, n - 1) * CHUNK
                        q_at = QA_AT + ((j % 2) * CHUNKS + n) * P
                        mm = products(out, [(wide(q_at, q_at + P), wide(k_at, k_at + P))], True, n > 0)
                        if n == 0:
                            mm = pe.matmul(out[:, CHUNK:P], ident_bf[:, :], all_masked[:, :],
                                           start=False, stop=True)
                    mm.then_inc(w_scored, 1)

                def turn(j, half):
                    pe.wait_ge(w_p_ready, j + 1)
                    if j:
                        pe.wait_ge(w_pt_ready, 2 * (j - 1) + half + 1)
                    for k in range(HALF):
                        a = (HALF * half + k) * P
                        mm = pe.transpose(bank[4 + half][:, k * P:(k + 1) * P], wprob[j % 2][:, a:a + P], ident[:, :])
                    mm.then_inc(w_turned, 1)

                def value(j, half):
                    pe.wait_ge(w_pt_ready, 2 * j + half + 1)
                    if j == 0:
                        pe.wait_ge(v_moved, 1)
                    if j:
                        pe.wait_ge(w_o_ready, 2 * (j - 1) + half + 1)
                    for n in range(HALF * half, HALF * (half + 1)):
                        v_at = V_AT + n // 2 * P if n % 2 or n == 0 else VS_AT + (n // 2 - 1) * P
                        v_at += j // GROUP_PAIRS * DH
                        p_at = PT_AT + half * SEQ + (n % HALF) * P
                        mm = products(bank[6 + half][0:DH, (n % HALF) * P:(n % HALF + 1) * P],
                                      [(wide(v_at, v_at + DH), wide(p_at, p_at + P))], True, True)
                    mm.then_inc(w_pv_done, 1)

                def fillers(n):
                    for j in range(PAIRS):
                        free_at = (w_q_scaled, j - 1) if j > 1 else (w_k_scaled, 1) if j else None
                        yield from project(n + j, j % 2, free_at)
                    yield from out_pair(n + PAIRS, w_q_scaled, PAIRS, w_o_ready, 2)

                fill = fillers(n)
                n += PAIRS + len(WO_KBS)

                def f(steps):
                    for _ in range(steps):
                        next(fill, None)

                f(4)
                row_sums(nn)
                f(KB)
                pe.wait_ge(w_v_biased, 1)
                for t in range(TB):
                    mm = pe.transpose(bank[7][:, t * P:(t + 1) * P], sq[:, 0, t * P:(t + 1) * P], ident[:, :])
                mm.then_inc(w_v_turned, 1)
                for j in range(PAIRS + 1):
                    before, after_0, after_1, between, end = {PAIRS - 2: (1, 1, 2, 1, 0), PAIRS - 1: (1, 1, 1, 1, 0),
                                                              PAIRS: (1, 0, 0, 1, 0)}.get(j, (1, 1, 2, 2, 2))
                    f(before)
                    if j < PAIRS:
                        if j % GROUP_PAIRS == 0:
                            pe.wait_ge(w_k_ready, j // GROUP_PAIRS + 1)
                        pe.wait_ge(w_q_ready, j + 1)
                        score(j, 0)
                    f(after_0)
                    if j:
                        turn(j - 1, 0)
                    if j < PAIRS:
                        score(j, 1)
                    f(after_1)
                    if j:
                        turn(j - 1, 1)
                        value(j - 1, 0)
                    f(between)
                    if j:
                        value(j - 1, 1)
                    f(end)
                for _ in fill:
                    pass
                out_stage(n - len(WO_KBS), nn + 1, WO_KBS, O_AT, first_done=True)

            ffn(0, 0)
            fox(1)
            ffn(1, 2)
            ffn(2, 3)
            window(4)
            ffn(3, 5)
            for half_d in range(2):
                for t in range(TB):
                    if half_d == 1 and t == TB - 1:
                        pe.wait_ge(ms_ready, 7)
                    for k in range(4):
                        m = 4 * half_d + k
                        if t == 0:
                            pe.wait_ge(h_ready, 8 * 6 + m + 1)
                        if t == 0 and half_d == 1 and k == 3:
                            token_sums(6, 7)
                        mm = pe.transpose(bank[4 * half_d + t][:, k * P:(k + 1) * P],
                                          h[:, m * SEQ + t * P:m * SEQ + (t + 1) * P], ident[:, :])
                    mm.then_inc(y_turned, 1)

        @block.scalar
        def _(act):
            act.dma_start(gain[:, :], gains).then_inc(small_loaded, 16)
            act.dma_start(bf[:, :], fox_b).then_inc(small_loaded, 16)
            act.dma_start(bq[:, :], swa_bq).then_inc(small_loaded, 16)
            act.dma_start(bk[:, :], swa_bk).then_inc(small_loaded, 16)
            act.dma_start(bv[:, :], swa_bv).then_inc(small_loaded, 16)
            for par in range(2):
                act.dma_start(sink[64 * par:64 * par + 64, :], sinks[par:par + 1, :].to_broadcast([64, PAIRS]))\
                   .then_inc(small_loaded, 16)

            def split_hi(n, r, base, cols, count=None):
                act.wait_ge(raw_loaded[(base + r) % RAW], count)
                slot = (base + r) % SPLIT
                act.activation(w_hi[:, slot, 0:cols], raw[:, (base + r) % RAW, 0:cols], ACT.Copy)\
                   .then_inc(w_hi_ready, 1)

            def split_next(used, base, r, turn_of, cols=UNIT):
                act.wait_ge(unit_used, used)
                q = r + LOOK
                split_hi(None, q, base, cols, 16 * (turn_of + (base + q) // RAW + 1))

            def post_block(nn, i4, r, first=False):
                m_at = (i4 + r) * SEQ
                if not first:
                    act.wait_ge(acc_ready, 9 * nn + i4 + r)
                act.wait_ge(h_ready, 8 * nn + i4 + r + 1)
                if nn < 6:
                    act.activation(dyn(u_hi, m_at), dyn(h, m_at), ACT.Copy,
                                   scale=gain[:, bass.ds(8 * nn + i4 + r, 1)]).then_inc(u_hi_ready, 1)
                act.activation(sq[:, r % 2, :], dyn(h, m_at), ACT.Square).then_inc(sq_ready, 1)

            act.wait_ge(small_loaded, 16 * 7)
            for n in range(LOOK):
                split_hi(n, n, 0, UNIT, 16)
            for m in range(KB):
                post_block(0, m - m % 2, m % 2, m == 0)
            act.wait_ge(x_turned, KB)
            act.dma_start(final_gb[:, :], final_g.to_broadcast([P, D])).then_inc(final_g_loaded, 16)

            def row_copy(nn):
                act.wait_ge(row_sum, nn + 1)
                act.activation(rstd_row[:, :], bank[5][:, :], ACT.Copy).then_inc(row_ready, 1)

            def ffn(f, nn, last):
                base = FFN_BASE[f]

                def in_body(i):
                    for r in range(IN_UNITS):
                        split_next(base + 4 * i + r + 1, base, r, i)
                        if type(i) is int and r == 2:
                            row_copy(nn)
                        if r == 2:
                            for c in range(2):
                                act.wait_ge(gate_scaled, FB * f + 2 * i + c + 1)
                                act.activation(silu_buf[:, c * SEQ:(c + 1) * SEQ],
                                               g_scaled_buf[:, c * SEQ:(c + 1) * SEQ], ACT.Silu)\
                                   .then_inc(silu_ready, 1)
                        if r == 3:
                            for c in range(2):
                                act.wait_ge(prod_ready, FB * f + 2 * i + c + 1)
                                act.activation(dyn(wide_hi, 2 * SEQ * i + c * SEQ),
                                               up_buf[:, c * SEQ:(c + 1) * SEQ], ACT.Copy)\
                                   .then_inc(a_hi_ready, 1)

                in_body(0)
                with act.Fori(1, IN_BODIES) as i:
                    in_body(i)
                out_stage(base + IN_BODIES * IN_UNITS, nn + 1, OUT_KBS, OUT_COLS, last)

            def out_stage(base, nn, kbs, cols, last=False, first_split=False):
                units = 2 * len(kbs)

                def body(i):
                    for r in range(units):
                        if first_split and i == 0 and r == 0:
                            continue
                        if not (last and type(i) is int and i == OUT_BODIES - 1 and r + LOOK >= units):
                            split_next(base + units * i + r + 1, base, r, units // RAW * i,
                                       cols if r + LOOK < units else UNIT)
                        if r % len(kbs) == len(kbs) - 1:
                            mp = r // len(kbs)
                            for c in range(2):
                                post_block(nn, 4 * i, 2 * mp + c)

                if last or first_split:
                    for i in range(OUT_BODIES):
                        body(i)
                else:
                    with act.Fori(0, OUT_BODIES) as i:
                        body(i)

            def step(n):
                split_next(n + 1, n, 0, 0)

            def project_hi(count, j, is_q):
                act.wait_ge(qk_scaled, count)
                if is_q:
                    a = (j % 2) * SEQ
                    act.activation(wide_hi[0:64, QA_AT + a:QA_AT + a + SEQ], scaled[0:64, :], ACT.Copy)
                    last = act.activation(wide_hi[64:128, QB_AT + a:QB_AT + a + SEQ], scaled[64:128, :], ACT.Copy)
                else:
                    a = K_AT + (j % 2) * SEQ
                    last = act.activation(wide_hi[:, a:a + SEQ], scaled[:, :], ACT.Copy)
                last.then_inc(qk_hi_ready, 1)

            def fox(nn):
                n = FOX_BASE
                step(n)
                n += 1
                step(n)
                n += 1
                row_copy(nn)
                act.wait_ge(consts, 1)
                act.wait_ge(f_chain, 3)
                act.activation(scratch[0:HEADS, 512:1024], scratch[0:HEADS, 512:1024], ACT.Exp, scale=-1.0)\
                   .then_inc(f_act, 1)
                act.wait_ge(f_act, 1)
                act.activation(scratch[0:HEADS, 512:1024], scratch[0:HEADS, 512:1024], ACT.Ln,
                               bias=ones[0:HEADS, 0:1]).then_inc(f_act, 1)
                for k in range(1, V_UNITS):
                    step(n)
                    n += 1
                    if k == 1:
                        act.wait_ge(f_chain, 7)
                        act.activation(decay[0:HEADS, :], scratch[0:HEADS, 0:512], ACT.Copy)\
                           .then_inc(f_act, 1)
                    if k % 4 == 3:
                        for t in range(TB):
                            act.wait_ge(rstd_ready, nn + 1)
                            a = V_AT + t * D + (k // 4) * 512
                            act.activation(wide_hi[:, a:a + 512], bank[4 * (k // 4) + t][:, :], ACT.Copy,
                                           scale=rstd[:, t:t + 1]).then_inc(v_hi_ready, 1)
                for k in range(2):
                    step(n)
                    n += 1
                    if k == 0:
                        act.wait_ge(zeroed, 4)
                    project_hi(k + 1, 0, k == 0)

                for t in range(HEADS + 1):
                    j = t // 2
                    b = t % 2

                    def pt_hi(kb):
                        at = TB * (t - 1) + kb
                        cols = SEQ - kb * P
                        act.wait_ge(turned, at + 1)
                        if at >= 2:
                            act.wait_ge(pv_done, at - 1)
                        a = PT_AT + (at % 2) * SEQ
                        act.activation(wide_hi[:, a:a + cols], bank[5 + at % 2][:, 0:cols], ACT.Copy)\
                           .then_inc(pt_hi_ready, 1)

                    def exp(i):
                        nk = FOX_KEYS[i]
                        act.wait_ge(nmax_ready, TB * t + (TB if i < 2 else ORDER.index(i) + 1))
                        act.activation(prob[b][:, FOX_P_AT[i]:FOX_P_AT[i] + nk],
                                       bank[FOX_BANK[i]][:, FOX_BANK_AT[i]:FOX_BANK_AT[i] + nk], ACT.Exp,
                                       bias=nmax[:, b, i:i + 1], accum_out=psum_p[:, b, i:i + 1])\
                           .then_inc(expd, 1)

                    if t:
                        pt_hi(0)
                    if t < HEADS:
                        if t >= 2:
                            act.wait_ge(turned, TB * (t - 1))
                            act.wait_ge(rsum_ready, t - 1)
                        exp(3)
                        exp(2)
                    if t:
                        pt_hi(1)
                    if t < HEADS:
                        exp(0)
                        exp(1)
                    if j + 1 < PAIRS:
                        if j >= 1:
                            act.wait_ge(scored, TB * 2 * j)
                        project_hi(t + 3, j + 1, b == 0)
                    if t:
                        pt_hi(2)
                        pt_hi(3)
                    if t:
                        par, jo = (t - 1) % 2, (t - 1) // 2
                        act.wait_ge(pv_done, TB * t)
                        act.activation(wide_hi[64 * par:64 * par + 64, O_AT + jo * SEQ:O_AT + (jo + 1) * SEQ],
                                       bank[7][0:DH, :], ACT.Copy).then_inc(o_hi_ready, 1)
                    if j + 1 < PAIRS or t == HEADS - 1:
                        step(n)
                        n += 1
                out_stage(n - 1, nn + 1, WO_KBS, UNIT, first_split=True)

            def window_q_hi(j):
                act.wait_ge(w_q_scaled, j + 1)
                for par in range(2):
                    rows = slice(64 * par, 64 * par + 64)
                    last = act.activation(window_q(wide_hi, par, j % 2 * CHUNKS, CHUNKS), chunks(scaled[rows, :]),
                                          ACT.Identity, bias=bq_scaled[rows, j:j + 1])
                last.then_inc(w_q_hi_ready, 1)

            def window_k_hi(g):
                act.wait_ge(w_k_scaled, 1)
                rows = slice(64 * g, 64 * g + 64)
                for to in (g, 1 - g):
                    last = act.activation(wide_hi[64 * to:64 * to + 64, K_AT + g * SEQ:K_AT + (g + 1) * SEQ],
                                          sq[rows, 1, :], ACT.Identity, bias=bk[rows, :])
                last.then_inc(w_k_hi_ready, 1)

            def window_v_hi():
                act.wait_ge(w_v_turned, 1)
                act.activation(wide_hi[:, V_AT:V_AT + SEQ], bank[7][:, :], ACT.Copy).then_inc(w_v_hi_ready, 1)
                act.wait_ge(w_v_hi_ready, 1)
                act.activation(wide_hi[0:64, VS_AT:VS_AT + 3 * P], f32(wide_hi[64:128, V_AT:V_AT + 3 * P]), ACT.Copy)
                act.activation(wide_hi[64:128, VS_AT:VS_AT + 3 * P], f32(wide_hi[0:64, V_AT + P:V_AT + 4 * P]),
                               ACT.Copy).then_inc(v_moved_hi, 1)

            def window(nn):
                n = SWA_BASE
                for _ in range(2):
                    step(n)
                    n += 1
                act.wait_ge(zeroed, 8)
                act.wait_ge(biases_ready, 1)
                row_copy(nn)
                window_k_hi(0)
                step(n)
                n += 1
                window_q_hi(0)

                for j in range(PAIRS + 1):
                    b = j % 2

                    def exps(half):
                        act.wait_ge(w_nmax_ready, 2 * j + half + 1)
                        if half == 0 and j >= 2:
                            act.wait_ge(w_turned, 2 * (j - 1))
                            act.wait_ge(w_rsum_ready, j - 1)
                        for c in range(HALF * half, HALF * (half + 1)):
                            act.activation(wprob[b][:, c * P:(c + 1) * P],
                                           bank[2 + half][:, (c % HALF) * P:(c % HALF + 1) * P], ACT.Exp,
                                           bias=wmax[:, b, c:c + 1], accum_out=wsum[:, b, c:c + 1])\
                               .then_inc(w_expd, 1)

                    def pt_hi(half):
                        act.wait_ge(w_turned, 2 * (j - 1) + half + 1)
                        if j >= 2:
                            act.wait_ge(w_pv_done, 2 * (j - 2) + half + 1)
                        a = PT_AT + half * SEQ
                        act.activation(wide_hi[:, a:a + SEQ], bank[4 + half][:, :], ACT.Copy)\
                           .then_inc(w_pt_hi_ready, 1)

                    def o_hi(j, half):
                        act.wait_ge(w_pv_done, 2 * j + half + 1)
                        a = O_AT + j * SEQ + half * HALF * CHUNK
                        for par in range(2):
                            last = act.activation(chunks(wide_hi[64 * par:64 * par + 64, a:a + HALF * CHUNK]),
                                                  pair_output(bank[6 + half], par), ACT.Copy)
                        last.then_inc(w_o_hi_ready, 1)

                    if j >= 2:
                        o_hi(j - 2, 1)
                    if j < PAIRS:
                        exps(0)
                    if j:
                        pt_hi(0)
                    if j < PAIRS:
                        exps(1)
                        act.activation(esink[:, b, :], wmax[:, b, :], ACT.Exp, bias=sink[:, j:j + 1])\
                           .then_inc(w_esink_ready, 1)
                    if j:
                        pt_hi(1)
                    if j + 1 < PAIRS:
                        if j >= 1:
                            act.wait_ge(w_scored, 2 * j)
                        window_q_hi(j + 1)
                    if j:
                        o_hi(j - 1, 0)
                    if j == 0:
                        window_v_hi()
                        window_k_hi(1)
                    if j != PAIRS - 1:
                        step(n)
                        n += 1
                o_hi(PAIRS - 1, 1)
                out_stage(n - 1, nn + 1, WO_KBS, UNIT, first_split=True)

            ffn(0, 0, False)
            fox(1)
            ffn(1, 2, False)
            ffn(2, 3, False)
            window(4)
            ffn(3, 5, True)

        @block.vector
        def _(dve):
            def split_lo(n_mod, count, cols=UNIT):
                dve.wait_ge(w_hi_ready, count)
                s, r = n_mod % SPLIT, n_mod % RAW
                dve.tensor_tensor(w_lo[:, s, 0:cols], raw[:, r, 0:cols], f32(w_hi[:, s, 0:cols]),
                                  ALU.subtract).then_inc(w_ready, 1)

            def residual(nn, i4, r, src, scale):
                m_at = (i4 + r) * SEQ
                if scale is None:
                    dve.tensor_copy(dyn(h, m_at), src).then_inc(h_ready, 1)
                else:
                    dve.scalar_tensor_tensor(out=dyn(h, m_at), in0=src, scalar=scale, in1=dyn(h, m_at),
                                             op0=ALU.mult, op1=ALU.add).then_inc(h_ready, 1)

            def post_block(nn, i4, r):
                m_at = (i4 + r) * SEQ
                if nn < 6:
                    dve.wait_ge(u_hi_ready, 8 * nn + i4 + r + 1)
                    dve.scalar_tensor_tensor(out=dyn(u_lo, m_at), in0=dyn(h, m_at),
                                             scalar=gain[:, bass.ds(8 * nn + i4 + r, 1)],
                                             in1=f32(dyn(u_hi, m_at)), op0=ALU.mult, op1=ALU.subtract)\
                       .then_inc(u_ready, 1)
                dve.wait_ge(sq_ready, 8 * nn + i4 + r + 1)
                dve.wait_ge(acc_ready, 9 * nn + i4 + r + 1)
                dve.tensor_tensor(acc[:, :], acc[:, :], sq[:, r % 2, :], ALU.add).then_inc(acc_ready, 1)

            def mean_squares(nn, b):
                dve.wait_ge(tok_sum, nn + 1)
                dve.tensor_scalar(ms[:, :], bank[b][:, 0:2 * TB].rearrange("p (t two) -> p t two", two=2)[:, :, 0],
                                  1.0 / D, RMS_EPS, ALU.mult, ALU.add).then_inc(ms_ready, 1)
                if nn < 6:
                    dve.memset(acc[:, :], 0.0).then_inc(acc_ready, 1)

            def diagonals(nn):
                dve.wait_ge(rstd_ready, nn + 1)
                for t in range(TB):
                    last = dve.tensor_scalar(diag[:, t * P:(t + 1) * P], ident[:, :], rstd[:, t:t + 1], None,
                                             ALU.mult)
                last.then_inc(diag_ready, 1)

            dve.memset(acc[:, :], 0.0).then_inc(acc_ready, 1)
            dve.wait_ge(small_loaded, 16 * 7)
            dve.tensor_scalar(nsink[:, :], sink[:, :], -1.0, None, ALU.mult)
            dve.tensor_scalar(bq_scaled[:, :], bq[:, :], QSCALE, None, ALU.mult).then_inc(biases_ready, 1)
            for n in range(LOOK):
                split_lo(n, n + 1)
            for m in range(KB):
                dve.wait_ge(x_turned, m + 1)
                residual(0, m, 0, bank[4 + m % 4][:, :], None)
            for m in range(KB):
                post_block(0, m - m % 2, m % 2)
            dve.wait_ge(consts, 1)
            dve.tensor_copy(pick_r[:, :], pick[:, :])

            def ffn(f, nn, last):
                base = FFN_BASE[f]

                def in_body(i):
                    first = type(i) is int
                    for r in range(IN_UNITS):
                        split_lo(base + r + LOOK, base + 4 * i + r + LOOK + 1)
                        if first and r == 1:
                            mean_squares(nn, 5)
                            diagonals(nn)
                        if r == (2 if first else 1):
                            dve.wait_ge(unit_used, base + 4 * i + 2)
                            if first:
                                dve.wait_ge(row_ready, nn + 1)
                            for c in range(2):
                                dve.tensor_tensor(g_scaled_buf[:, c * SEQ:(c + 1) * SEQ], bank[c][:, :],
                                                  rstd_row[:, :], ALU.mult).then_inc(gate_scaled, 1)
                        if r == 3:
                            dve.wait_ge(unit_used, base + 4 * i + 4)
                            for c in range(2):
                                dve.tensor_tensor(up_buf[:, c * SEQ:(c + 1) * SEQ], bank[2 + c][:, :],
                                                  rstd_row[:, :], ALU.mult).then_inc(up_scaled, 1)
                            for c in range(2):
                                up = up_buf[:, c * SEQ:(c + 1) * SEQ]
                                dve.wait_ge(silu_ready, FB * f + 2 * i + c + 1)
                                dve.wait_ge(up_scaled, FB * f + 2 * i + c + 1)
                                dve.tensor_tensor(up, up, silu_buf[:, c * SEQ:(c + 1) * SEQ], ALU.mult)\
                                   .then_inc(prod_ready, 1)
                            for c in range(2):
                                dve.wait_ge(a_hi_ready, FB * f + 2 * i + c + 1)
                                dve.tensor_tensor(dyn(wide_lo, 2 * SEQ * i + c * SEQ),
                                                  up_buf[:, c * SEQ:(c + 1) * SEQ],
                                                  f32(dyn(wide_hi, 2 * SEQ * i + c * SEQ)), ALU.subtract)\
                                   .then_inc(a_ready, 1)

                in_body(0)
                with dve.Fori(1, IN_BODIES) as i:
                    in_body(i)
                out_stage(base + IN_BODIES * IN_UNITS, nn + 1, OUT_KBS, 0.5, OUT_COLS, last)

            def out_stage(base, nn, kbs, scale, cols, last=False, first_split=False):
                units = 2 * len(kbs)

                def body(i):
                    for r in range(units):
                        if first_split and i == 0 and r == 0:
                            continue
                        if not (last and type(i) is int and i == OUT_BODIES - 1 and r + LOOK >= units):
                            split_lo(base + r + LOOK, base + units * i + r + LOOK + 1,
                                     cols if r + LOOK < units else UNIT)
                        if r % len(kbs) == len(kbs) - 1:
                            mp = r // len(kbs)
                            dve.wait_ge(unit_used, base + units * i + r + 1)
                            first_bank = 0 if first_split and i == 0 and mp == 0 else 4 + 2 * mp
                            for c in range(2):
                                residual(nn, 4 * i, 2 * mp + c, bank[first_bank + c][:, :], scale)
                            for c in range(2):
                                post_block(nn, 4 * i, 2 * mp + c)

                if last or first_split:
                    for i in range(OUT_BODIES):
                        body(i)
                else:
                    with dve.Fori(0, OUT_BODIES) as i:
                        body(i)

            def step(n):
                split_lo(n + LOOK, n + LOOK + 1)

            def fox(nn):
                n = FOX_BASE
                x0, x1, x2, x3 = (scratch[0:HEADS, 512 * k:512 * k + 512] for k in range(4))
                step(n)
                n += 1
                mean_squares(nn, 5)
                step(n)
                n += 1
                diagonals(nn)
                dve.wait_ge(row_ready, nn + 1)
                dve.wait_ge(unit_used, FOX_BASE + 2)
                dve.tensor_tensor(x0, bank[4][0:HEADS, :], rstd_row[0:HEADS, :], ALU.mult).then_inc(f_chain, 1)
                dve.wait_ge(f_chain, 1)
                dve.tensor_scalar(x0, x0, bf[:, 0:1], None, ALU.add).then_inc(f_chain, 1)
                dve.wait_ge(f_chain, 2)
                dve.scalar_tensor_tensor(out=x1, in0=x0, scalar=-1.0, in1=x0, op0=ALU.mult, op1=ALU.max)\
                   .then_inc(f_chain, 1)
                dve.tensor_scalar(x3, x0, 0.0, None, ALU.min).then_inc(f_chain, 1)
                for k in range(1, V_UNITS):
                    step(n)
                    if k == 1:
                        dve.wait_ge(f_act, 2)
                        dve.wait_ge(f_chain, 4)
                        dve.tensor_tensor(x2, x1, x3, ALU.subtract).then_inc(f_chain, 1)
                        dve.wait_ge(f_chain, 5)
                        dve.memset(x3, 1.0).then_inc(f_chain, 1)
                        dve.wait_ge(f_chain, 6)
                        dve.tensor_tensor_scan(x0, x3, x2, 0.0, ALU.mult, ALU.add).then_inc(f_chain, 1)
                    if k == 2:
                        dve.wait_ge(f_act, 3)
                        dve.tensor_tensor(decay[32:32 + HEADS, :], x0, f32(decay[0:HEADS, :]), ALU.subtract)\
                           .then_inc(decay_ready, 1)
                    n += 1
                    if k % 4 == 3:
                        for t in range(TB):
                            dve.wait_ge(v_hi_ready, TB * (k // 4) + t + 1)
                            a = V_AT + t * D + (k // 4) * 512
                            dve.scalar_tensor_tensor(out=wide_lo[:, a:a + 512], in0=bank[4 * (k // 4) + t][:, :],
                                                     scalar=rstd[:, t:t + 1], in1=f32(wide_hi[:, a:a + 512]),
                                                     op0=ALU.mult, op1=ALU.subtract).then_inc(v_ready, 1)

                def project_scaled(n, is_q, count):
                    if count:
                        dve.wait_ge(qk_ready, count)
                    dve.wait_ge(unit_used, n + 1)
                    if is_q:
                        dve.scalar_tensor_tensor(out=scaled, in0=bank[0][:, :], scalar=QSCALE, in1=rstd_row[:, :],
                                                 op0=ALU.mult, op1=ALU.mult).then_inc(qk_scaled, 1)
                    else:
                        dve.tensor_tensor(scaled, bank[1][:, :], rstd_row[:, :], ALU.mult).then_inc(qk_scaled, 1)

                def project_lo(count, j, is_q):
                    dve.wait_ge(qk_hi_ready, count)
                    if is_q:
                        a = (j % 2) * SEQ
                        for at, rows in ((QA_AT + a, slice(0, 64)), (QB_AT + a, slice(64, 128))):
                            last = dve.tensor_tensor(wide_lo[rows, at:at + SEQ], scaled[rows, :],
                                                     f32(wide_hi[rows, at:at + SEQ]), ALU.subtract)
                        last.then_inc(qk_ready, 1)
                    else:
                        a = K_AT + (j % 2) * SEQ
                        dve.tensor_tensor(wide_lo[:, a:a + SEQ], scaled, f32(wide_hi[:, a:a + SEQ]),
                                          ALU.subtract).then_inc(qk_ready, 1)

                for k in range(2):
                    step(n)
                    project_scaled(n, k == 0, k)
                    n += 1
                    project_lo(k + 1, 0, k == 0)

                for t in range(HEADS + 1):
                    j = t // 2
                    b = t % 2

                    def pt_lo(kb):
                        at = TB * (t - 1) + kb
                        cols = SEQ - kb * P
                        a = PT_AT + (at % 2) * SEQ
                        dve.wait_ge(pt_hi_ready, at + 1)
                        dve.tensor_tensor(wide_lo[:, a:a + cols], bank[5 + at % 2][:, 0:cols],
                                          f32(wide_hi[:, a:a + cols]), ALU.subtract).then_inc(pt_ready, 1)

                    def row_max(i):
                        dve.wait_ge(scored, TB * t + (TB if i < 2 else ORDER.index(i) + 1))
                        dve.tensor_reduce(nmax[:, b, i:i + 1],
                                          bank[FOX_BANK[i]][:, FOX_BANK_AT[i]:FOX_BANK_AT[i] + FOX_KEYS[i]],
                                          AX_X, ALU.max, negate=True).then_inc(nmax_ready, 1)

                    if t < HEADS:
                        if t >= 2:
                            dve.wait_ge(expd, TB * (t - 1))
                        row_max(3)
                        row_max(2)
                    if t:
                        pt_lo(0)
                    if t < HEADS:
                        row_max(0)
                        row_max(1)
                    if j + 1 < PAIRS:
                        project_scaled(n, b == 0, t + 2)
                    if t:
                        pt_lo(1)
                        pt_lo(2)
                    if j + 1 < PAIRS:
                        project_lo(t + 3, j + 1, b == 0)
                    if t:
                        pt_lo(3)
                    if t < HEADS:
                        dve.wait_ge(expd, TB * (t + 1))
                        dve.reciprocal(rsum[:, b, :], psum_p[:, b, :]).then_inc(rsum_ready, 1)
                        dve.wait_ge(rsum_ready, t + 1)
                        for i in ORDER:
                            part = prob[b][:, FOX_P_AT[i]:FOX_P_AT[i] + FOX_KEYS[i]]
                            last = dve.tensor_scalar(part, part, rsum[:, b, i:i + 1], None, ALU.mult)
                        last.then_inc(p_ready, 1)
                    if t:
                        par, jo = (t - 1) % 2, (t - 1) // 2
                        rows = slice(64 * par, 64 * par + 64)
                        a = O_AT + jo * SEQ
                        dve.wait_ge(o_hi_ready, t)
                        dve.tensor_tensor(wide_lo[rows, a:a + SEQ], bank[7][0:DH, :], f32(wide_hi[rows, a:a + SEQ]),
                                          ALU.subtract).then_inc(o_ready, 1)
                    if j + 1 < PAIRS or t == HEADS - 1:
                        step(n)
                        n += 1
                out_stage(n - 1, nn + 1, WO_KBS, 1.0, UNIT, first_split=True)

            def window_q_lo(j):
                dve.wait_ge(w_q_hi_ready, j + 1)
                for par in range(2):
                    rows = slice(64 * par, 64 * par + 64)
                    last = dve.scalar_tensor_tensor(out=window_q(wide_lo, par, j % 2 * CHUNKS, CHUNKS),
                                                    in0=chunks(scaled[rows, :]), scalar=bq_scaled[rows, j:j + 1],
                                                    in1=f32(window_q(wide_hi, par, j % 2 * CHUNKS, CHUNKS)),
                                                    op0=ALU.add, op1=ALU.subtract)
                last.then_inc(w_q_ready, 1)

            def window_k_lo(g):
                dve.wait_ge(w_k_hi_ready, g + 1)
                rows = slice(64 * g, 64 * g + 64)
                a = K_AT + g * SEQ
                for to in (g, 1 - g):
                    last = dve.scalar_tensor_tensor(out=wide_lo[64 * to:64 * to + 64, a:a + SEQ], in0=sq[rows, 1, :],
                                                    scalar=bk[rows, :], in1=f32(wide_hi[rows, a:a + SEQ]),
                                                    op0=ALU.add, op1=ALU.subtract)
                last.then_inc(w_k_ready, 1)

            def window_v_lo():
                dve.wait_ge(w_v_hi_ready, 1)
                dve.tensor_tensor(wide_lo[:, V_AT:V_AT + SEQ], bank[7][:, :], f32(wide_hi[:, V_AT:V_AT + SEQ]),
                                  ALU.subtract).then_inc(w_v_ready, 1)
                dve.wait_ge(w_v_ready, 1)
                dve.wait_ge(v_moved_hi, 1)
                dve.tensor_copy(wide_lo[0:64, VS_AT:VS_AT + 3 * P], f32(wide_lo[64:128, V_AT:V_AT + 3 * P]))
                dve.tensor_copy(wide_lo[64:128, VS_AT:VS_AT + 3 * P], f32(wide_lo[0:64, V_AT + P:V_AT + 4 * P]))\
                   .then_inc(v_moved, 1)

            def window(nn):
                n = SWA_BASE
                for _ in range(2):
                    step(n)
                    n += 1
                mean_squares(nn, 5)
                diagonals(nn)
                dve.wait_ge(biases_ready, 1)
                dve.wait_ge(row_ready, nn + 1)
                dve.tensor_tensor(sq[:, 1, :], bank[1][:, :], rstd_row[:, :], ALU.mult).then_inc(w_k_scaled, 1)
                dve.tensor_tensor(sq[:, 0, :], bank[2][:, :], rstd_row[:, :], ALU.mult).then_inc(w_v_scaled, 1)

                def project_scaled(n, j):
                    if j:
                        dve.wait_ge(w_q_ready, j)
                    dve.wait_ge(unit_used, n + 1)
                    dve.scalar_tensor_tensor(out=scaled, in0=bank[j % 2][:, :], scalar=QSCALE, in1=rstd_row[:, :],
                                             op0=ALU.mult, op1=ALU.mult).then_inc(w_q_scaled, 1)

                window_k_lo(0)
                project_scaled(n, 0)
                dve.wait_ge(w_v_scaled, 1)
                dve.tensor_scalar(sq[:, 0, :], sq[:, 0, :], bv[:, 0:1], None, ALU.add).then_inc(w_v_biased, 1)
                window_q_lo(0)
                step(n)
                n += 1

                for j in range(PAIRS + 1):
                    b = j % 2

                    def row_max(half):
                        if half == 0 and j >= 2:
                            dve.wait_ge(w_esink_ready, j - 1)
                        dve.wait_ge(w_scored, 2 * j + half + 1)
                        part = wmax[:, b, HALF * half:HALF * (half + 1)]
                        dve.tensor_reduce(part, bank[2 + half][:, :].rearrange("p (n k) -> p n k", k=P),
                                          AX_X, ALU.max, negate=True).then_inc(w_maxed, 1)
                        dve.wait_ge(w_maxed, 2 * j + half + 1)
                        dve.tensor_scalar(part, part, nsink[:, j:j + 1], None, ALU.min).then_inc(w_nmax_ready, 1)

                    def pt_lo(half):
                        a = PT_AT + half * SEQ
                        dve.wait_ge(w_pt_hi_ready, 2 * (j - 1) + half + 1)
                        dve.tensor_tensor(wide_lo[:, a:a + SEQ], bank[4 + half][:, :], f32(wide_hi[:, a:a + SEQ]),
                                          ALU.subtract).then_inc(w_pt_ready, 1)

                    def o_lo(j, half):
                        a = O_AT + j * SEQ + half * HALF * CHUNK
                        dve.wait_ge(w_o_hi_ready, 2 * j + half + 1)
                        for par in range(2):
                            rows = slice(64 * par, 64 * par + 64)
                            last = dve.tensor_tensor(chunks(wide_lo[rows, a:a + HALF * CHUNK]),
                                                     pair_output(bank[6 + half], par),
                                                     chunks(f32(wide_hi[rows, a:a + HALF * CHUNK])), ALU.subtract)
                        last.then_inc(w_o_ready, 1)

                    if j >= 2:
                        o_lo(j - 2, 1)
                    if j < PAIRS:
                        row_max(0)
                        row_max(1)
                    if j:
                        pt_lo(0)
                    if j + 1 < PAIRS:
                        project_scaled(n, j + 1)
                    if j:
                        pt_lo(1)
                    if j < PAIRS:
                        dve.wait_ge(w_expd, CHUNKS * (j + 1))
                        dve.wait_ge(w_esink_ready, j + 1)
                        dve.tensor_tensor(wsum[:, b, :], wsum[:, b, :], esink[:, b, :], ALU.add)\
                           .then_inc(w_sum_ready, 1)
                        dve.wait_ge(w_sum_ready, j + 1)
                        dve.reciprocal(wrsum[:, b, :], wsum[:, b, :]).then_inc(w_rsum_ready, 1)
                        dve.wait_ge(w_rsum_ready, j + 1)
                        part = wprob[b].rearrange("p (n k) -> p n k", k=P)
                        dve.tensor_tensor(part, part, wrsum[:, b, :].unsqueeze(2).to_broadcast([P, CHUNKS, P]),
                                          ALU.mult).then_inc(w_p_ready, 1)
                    if j + 1 < PAIRS:
                        window_q_lo(j + 1)
                    if j:
                        o_lo(j - 1, 0)
                    if j == 0:
                        window_v_lo()
                        window_k_lo(1)
                    if j != PAIRS - 1:
                        step(n)
                        n += 1
                o_lo(PAIRS - 1, 1)
                out_stage(n - 1, nn + 1, WO_KBS, 1.0, UNIT, first_split=True)

            ffn(0, 0, False)
            fox(1)
            ffn(1, 2, False)
            ffn(2, 3, False)
            window(4)
            ffn(3, 5, True)
            mean_squares(6, 7)
            dve.wait_ge(rstd_ready, 7)
            dve.wait_ge(final_g_loaded, 16)
            for n in range(2 * TB):
                t, half_d = n % TB, n // TB
                dve.wait_ge(y_turned, n + 1)
                dve.scalar_tensor_tensor(out=raw[:, n // 2, (n % 2) * 512:(n % 2 + 1) * 512], in0=bank[n][:, :],
                                         scalar=rstd[:, t:t + 1], in1=final_gb[:, half_d * 512:(half_d + 1) * 512],
                                         op0=ALU.mult, op1=ALU.mult).then_inc(y_scaled, 1)


def lay_out(inputs):
    a = {k: np.asarray(v) for k, v in inputs.items()}
    kb, pad = KB, np.zeros

    def columns(w, n):
        return w.reshape(kb, P, n, P).transpose(2, 1, 0, 3).reshape(n, P, UNIT)

    def wo(w):
        return w.reshape(2, 4, P, KB // 2, 256).transpose(3, 0, 2, 1, 4).reshape(WO_UNITS, P, UNIT)

    w_in = a["ffn_w_in"].reshape(4, 2, 4, P, 2, IN_BODIES, 256)
    ffn_in = w_in.transpose(0, 5, 4, 1, 3, 2, 6).reshape(4, IN_BODIES, IN_UNITS, P, UNIT)
    w_out = a["ffn_w_out"].reshape(4, FB, P, KB // 2, 256).transpose(0, 3, 2, 1, 4)
    ffn_out = pad((4, KB // 2, len(OUT_KBS), P, 3, 256), w_out.dtype)
    for u, kbs in enumerate(OUT_KBS):
        ffn_out[:, :, u, :, 0:len(kbs)] = w_out[:, :, :, kbs[0]:kbs[-1] + 1]
    ffn_out = ffn_out.reshape(4, KB // 2 * len(OUT_KBS) // RAW, RAW, P, OUT_COLS)

    fox = a["fox_w_in"][0]
    w_f = pad((1, P, UNIT), fox.dtype)
    w_f[0, :, 0:kb * HEADS] = fox[:, 3 * D:].reshape(kb, P, HEADS).transpose(1, 0, 2).reshape(P, kb * HEADS)
    w_v = fox[:, 2 * D:3 * D].reshape(4, 2, P, 2, 512).transpose(3, 0, 2, 1, 4).reshape(V_UNITS, P, UNIT)
    qk = np.stack([columns(fox[:, 0:D], PAIRS), columns(fox[:, D:2 * D], PAIRS)], 1).reshape(2 * PAIRS, P, UNIT)
    swa = a["swa_w_in"][0]
    kv = columns(swa[:, D:D + 2 * P], 2)
    mix_w = np.concatenate([w_v[0:1], w_f, w_v[1:], qk, wo(a["fox_w_o"][0]), kv, columns(swa[:, 0:D], PAIRS), wo(a["swa_w_o"][0])])
    b = a["swa_b_in"][0]
    return {
        "x": a["x"].reshape(SEQ, D),
        "gains": a["norm_g"].reshape(6, KB, P).transpose(2, 0, 1).reshape(P, 6 * KB),
        "final_g": a["final_g"].reshape(1, D),
        "ffn_in": ffn_in,
        "ffn_out": ffn_out,
        "mix_w": mix_w,
        "fox_b": a["fox_b_f"].reshape(HEADS, 1),
        "swa_bq": b[0:D].reshape(PAIRS, P).transpose(1, 0),
        "swa_bk": b[D:D + P].reshape(P, 1),
        "swa_bv": b[D + P:D + 2 * P].reshape(P, 1),
        "sinks": a["swa_sinks"].reshape(PAIRS, 2).transpose(1, 0),
    }


def kernel(**inputs):
    import concourse.bacc as bacc
    from concourse.bass_utils import run_bass_kernel_spmd

    nc = bacc.Bacc("TRN2", target_bir_lowering=False, num_devices=1)
    arrays = {k: np.ascontiguousarray(v) for k, v in lay_out(inputs).items()}
    args = {k: nc.dram_tensor(k + "_dram", v.shape, mybir.dt.from_np(v.dtype), kind="ExternalInput").ap()
            for k, v in arrays.items()}
    y = nc.dram_tensor("y_dram", (SEQ, D), F32, kind="ExternalOutput").ap()
    build(nc, y=y, **args)
    r = run_bass_kernel_spmd(nc, [{k + "_dram": v for k, v in arrays.items()}], core_ids=[0])
    return r.results[0]["y_dram"].reshape(1, SEQ, D)
```

```python
from contextlib import ExitStack

import numpy as np

import concourse.bass as bass
from concourse import mybir

F32 = mybir.dt.float32
F32R = mybir.dt.float32r
BF16 = mybir.dt.bfloat16
ALU = mybir.AluOpType
ACT = mybir.ActivationFunctionType
AX_X = mybir.AxisListType.X

P = 128
SEQ = 512
D = 1024
DFF = 2816
HEADS = 16
DH = 64
KV_HEADS = 2
TB = SEQ // P
KB = D // P
FB = DFF // P
PAIRS = HEADS // 2
RMS_EPS = 1e-6
QSCALE = DH ** -0.5
MASKED = -1e30

RAW = 4
SPLIT = 2
UNIT = 1024
LOOK = SPLIT

IN_BODIES = FB // 2
IN_UNITS = 4
OUT_KBS = [range(3 * u, 3 * u + 3) for u in range(6)] + [range(18, 20), range(20, 22)]
OUT_COLS = 3 * 256
OUT_BODIES = 2
WO_KBS = [range(0, 4), range(4, 8)]

FFN_UNITS = IN_BODIES * IN_UNITS + (KB // 2) * len(OUT_KBS)
WO_UNITS = (KB // 2) * len(WO_KBS)
V_UNITS = 8
FOX_UNITS = 1 + V_UNITS + 2 * PAIRS + WO_UNITS
SWA_UNITS = 2 + PAIRS + WO_UNITS
FFN_BASE = [0, FFN_UNITS + FOX_UNITS, 2 * FFN_UNITS + FOX_UNITS, 3 * FFN_UNITS + FOX_UNITS + SWA_UNITS]
MIX_BASE = [FFN_UNITS, 3 * FFN_UNITS + FOX_UNITS]


FOX_BASE, SWA_BASE = MIX_BASE

FOX_KEYS = [(i + 1) * P for i in range(TB)]
FOX_BANK = [2, 2, 3, 4]
FOX_BANK_AT = [0, P, 0, 0]
FOX_P_AT = [sum(FOX_KEYS[:i]) for i in range(TB)]

CHUNK = 64
CHUNKS = SEQ // CHUNK
HALF = CHUNKS // 2
GROUP_PAIRS = PAIRS // KV_HEADS

ORDER = (3, 2, 0, 1)


def build(nc, x, gains, ffn_in, ffn_out, mix_w, fox_b, swa_bq, swa_bk, swa_bv, sinks, y):
    ctx = ExitStack()
    with ctx:
        def sb(name, shape, dt=F32):
            return ctx.enter_context(nc.sbuf_tensor(name, shape, dt))

        def sem(name):
            return ctx.enter_context(nc.semaphore(name))

        h = sb("h", [P, KB * SEQ])
        u_hi = sb("u_hi", [P, KB * SEQ], F32R)
        u_lo = sb("u_lo", [P, KB * SEQ], F32R)
        wide_hi = sb("wide_hi", [P, 12288], F32R)
        wide_lo = sb("wide_lo", [P, 12288], F32R)
        V_AT, O_AT, PT_AT, K_AT, Q_AT = 0, 4096, 8192, 9216, 10240
        FOX_Q_AT = [[9216, 9216], [9728, 10240]]
        FOX_K_AT = [10752, 11264]
        raw = sb("raw", [P, RAW, UNIT])
        w_hi = sb("w_hi", [P, SPLIT, UNIT], F32R)
        w_lo = sb("w_lo", [P, SPLIT, UNIT], F32R)
        scratch = sb("scratch", [P, 6 * SEQ])
        x_last = sb("x_last", [P, D])
        rstd_row = sb("rstd_row", [P, SEQ])
        sq = sb("sq", [P, 2, SEQ])
        acc = sb("acc", [P, SEQ])
        diag = sb("diag", [P, SEQ])
        gain = sb("gain", [P, 7 * KB])
        ident = sb("ident", [P, P])
        ones = sb("ones", [P, P])
        ident_bf = sb("ident_bf", [P, P], BF16)
        causal = sb("causal", [P, P], BF16)
        all_masked = sb("all_masked", [P, CHUNK], BF16)
        ms = sb("ms", [P, TB])
        half = sb("half", [P, TB])
        rstd = sb("rstd", [P, TB])
        bf = sb("bf", [HEADS, 1])
        bq = sb("bq", [P, PAIRS])
        bq_scaled = sb("bq_scaled", [P, PAIRS])
        bk = sb("bk", [P, 1])
        bv = sb("bv", [P, 1])
        sink = sb("sink", [P, PAIRS])
        nsink = sb("nsink", [P, PAIRS])
        nmax = sb("nmax", [P, 2, TB])
        psum_p = sb("psum_p", [P, 2, TB])
        wmax = sb("wmax", [P, 2, CHUNKS])
        wsum = sb("wsum", [P, 2, CHUNKS])
        wrsum = sb("wrsum", [P, 2, CHUNKS])
        esink = sb("esink", [P, 2, CHUNKS])
        rsum = sb("rsum", [P, 2, TB])
        pick = sb("pick", [P, HEADS])
        decay = sb("decay", [P, SEQ], F32R)
        g_scaled_buf, silu_buf, up_buf = (scratch[:, 2 * n * SEQ:2 * (n + 1) * SEQ] for n in range(3))
        prob = [scratch[:, 0:1280], scratch[:, 1280:2560]]
        scaled = scratch[:, 2560:3072]
        wprob = [scratch[:, 0:CHUNKS * P], scratch[:, CHUNKS * P:2 * CHUNKS * P]]
        bank = [ctx.enter_context(nc.psum_tensor(f"bank{b}", [P, 512], F32)) for b in range(8)]

        x_loaded = [sem(f"x_loaded{t}") for t in range(TB)]
        gain_loaded = sem("gain_loaded")
        small_loaded = sem("small_loaded")
        raw_loaded = [sem(f"raw_loaded{s}") for s in range(RAW)]
        w_hi_ready = sem("w_hi_ready")
        w_ready = sem("w_ready")
        unit_used = sem("unit_used")
        consts = sem("consts")
        consts_pool = sem("consts_pool")
        ident_ready = sem("ident_ready")
        x_turned = sem("x_turned")
        h_ready = sem("h_ready")
        u_hi_ready = sem("u_hi_ready")
        u_ready = sem("u_ready")
        sq_ready = sem("sq_ready")
        acc_ready = sem("acc_ready")
        tok_sum = sem("tok_sum")
        ms_ready = sem("ms_ready")
        rstd_ready = sem("rstd_ready")
        diag_ready = sem("diag_ready")
        row_sum = sem("row_sum")
        row_ready = sem("row_ready")
        gate_scaled = sem("gate_scaled")
        silu_ready = sem("silu_ready")
        up_scaled = sem("up_scaled")
        prod_ready = sem("prod_ready")
        a_hi_ready = sem("a_hi_ready")
        a_ready = sem("a_ready")
        f_chain = sem("f_chain")
        f_act = sem("f_act")
        decay_ready = sem("decay_ready")
        decay_placed = sem("decay_placed")
        picked = sem("picked")
        v_hi_ready = sem("v_hi_ready")
        v_ready = sem("v_ready")
        zeroed = sem("zeroed")
        qk_scaled = sem("qk_scaled")
        qk_hi_ready = sem("qk_hi_ready")
        qk_copied = sem("qk_copied")
        qk_ready = sem("qk_ready")
        scored = sem("scored")
        nmax_ready = sem("nmax_ready")
        biases_ready = sem("biases_ready")
        expd = sem("expd")
        rsum_ready = sem("rsum_ready")
        p_ready = sem("p_ready")
        turned = sem("turned")
        pt_hi_ready = sem("pt_hi_ready")
        pt_ready = sem("pt_ready")
        pv_done = sem("pv_done")
        o_hi_ready = sem("o_hi_ready")
        o_ready = sem("o_ready")
        w_v_scaled = sem("w_v_scaled")
        w_v_biased = sem("w_v_biased")
        w_v_turned = sem("w_v_turned")
        w_v_hi_ready = sem("w_v_hi_ready")
        w_v_ready = sem("w_v_ready")
        v_moved_hi = sem("v_moved_hi")
        v_moved = sem("v_moved")
        w_k_scaled = sem("w_k_scaled")
        w_k_hi_ready = sem("w_k_hi_ready")
        w_k_ready = sem("w_k_ready")
        w_q_scaled = sem("w_q_scaled")
        w_q_hi_ready = sem("w_q_hi_ready")
        w_q_copied = sem("w_q_copied")
        w_q_ready = sem("w_q_ready")
        w_scored = sem("w_scored")
        w_maxed = sem("w_maxed")
        w_nmax_ready = sem("w_nmax_ready")
        w_expd = sem("w_expd")
        w_esink_ready = sem("w_esink_ready")
        w_sum_ready = sem("w_sum_ready")
        w_rsum_ready = sem("w_rsum_ready")
        w_p_ready = sem("w_p_ready")
        w_turned = sem("w_turned")
        w_pt_hi_ready = sem("w_pt_hi_ready")
        w_pt_ready = sem("w_pt_ready")
        w_pv_done = sem("w_pv_done")
        w_o_hi_ready = sem("w_o_hi_ready")
        w_o_ready = sem("w_o_ready")
        y_turned = sem("y_turned")
        y_scaled_dve = sem("y_scaled_dve")
        y_scaled_act = sem("y_scaled_act")
        y_stored = sem("y_stored")

        def window_q(part, half, par, j):
            a = Q_AT + (j % 2) * CHUNKS * P
            return part[64 * half:64 * half + 64, a:a + CHUNKS * P]\
                .rearrange("p (n par q) -> p n par q", par=2, q=CHUNK)[:, :, par, :]

        def pair_output(b, par):
            return b[0:DH, :].rearrange("p (n par q) -> p n par q", par=2, q=CHUNK)[:, :, par, :]

        def beside(par):
            return slice(64 - 64 * par, 128 - 64 * par)

        def chunks(ap):
            return ap.rearrange("p (n c) -> p n c", c=CHUNK)

        def x_piece(g):
            piece = scratch[:, g * D:(g + 1) * D] if g < 3 else x_last[:, :]
            return piece.rearrange("p (t c) -> p t c", c=256)

        VS_AT = V_AT + SEQ

        block = ctx.enter_context(nc.Block())

        def blk(t, m, n=1):
            return t[:, m * SEQ:(m + n) * SEQ]

        def f32(ap):
            return ap.bitcast(F32)

        def dyn(t, start, size=SEQ):
            return t[:, bass.ds(start, size)]

        @block.sync
        def _(sp):
            def load_x(g):
                sp.dma_start(x_piece(g), x.rearrange("(t p) d -> p t d", p=P)[:, :, 2 * g * P:2 * (g + 1) * P])\
                  .then_inc(x_loaded[g], 16)

            def load_small():
                sp.dma_start(bf[:, :], fox_b).then_inc(small_loaded, 16)
                sp.dma_start(bq[:, :], swa_bq).then_inc(small_loaded, 16)
                sp.dma_start(bk[:, :], swa_bk).then_inc(small_loaded, 16)
                sp.dma_start(bv[:, :], swa_bv).then_inc(small_loaded, 16)
                for par in range(2):
                    sp.dma_start(sink[64 * par:64 * par + 64, :], sinks[par:par + 1, :].to_broadcast([64, PAIRS]))\
                      .then_inc(small_loaded, 16)

            def load(slot, src, cols, wait=None):
                if wait is not None:
                    sp.wait_ge(w_ready, wait)
                sp.dma_start(raw[:, slot, 0:cols], src).then_inc(raw_loaded[slot], 16)

            def load_ffn(f):
                base = FFN_BASE[f]

                def load_in(i):
                    for r in range(IN_UNITS):
                        first = f == 0 and type(i) is int
                        load((base + r) % RAW, ffn_in[f, i, r], UNIT,
                             None if first else base + 4 * i + r - RAW + 1)
                        if first:
                            for g in {0: (0,), 1: (1, 2, 3)}.get(r, ()):
                                load_x(g)
                            if r == IN_UNITS - 1:
                                load_small()

                load_in(0)
                with sp.Fori(1, IN_BODIES) as i:
                    load_in(i)
                out = base + IN_BODIES * IN_UNITS
                with sp.Fori(0, (KB // 2) * len(OUT_KBS) // RAW) as i:
                    for r in range(RAW):
                        load((out + r) % RAW, ffn_out[f, i, r], OUT_COLS, out + 4 * i + r - RAW + 1)

            def load_mixer(base, first, units):
                for n in range(units):
                    load((base + n) % RAW, mix_w[first + n], UNIT, base + n - RAW + 1)

            load_ffn(0)
            load_mixer(FOX_BASE, 0, FOX_UNITS)
            load_ffn(1)
            load_ffn(2)
            load_mixer(SWA_BASE, FOX_UNITS, SWA_UNITS)
            load_ffn(3)
            for n in range(2 * TB):
                t, half_d = n % TB, n // TB
                sp.wait_ge((y_scaled_dve, y_scaled_act)[n % 2], n // 2 + 1)
                sp.dma_start(y[t * P:(t + 1) * P, half_d * 512:(half_d + 1) * 512],
                             raw[:, n // 2, (n % 2) * 512:(n % 2 + 1) * 512]).then_inc(y_stored, 16)
            sp.wait_ge(y_stored, 16 * 2 * TB)

        @block.gpsimd
        def _(pool):
            def in_turn(k, ins, s):
                ins.then_inc(s, 1)
                pool.wait_ge(s, k)

            in_turn(1, pool.memset(ident[:, :], 0.0), consts_pool)
            in_turn(2, pool.affine_select(out=ident[:, :], in_=ident[:, :], compare_op=ALU.not_equal, fill=1.0,
                                          base=0, pattern=[[-1, P]], channel_multiplier=1), consts_pool)
            in_turn(1, pool.memset(ones[:, :], 1.0), ident_ready)
            in_turn(3, pool.memset(ident_bf[:, :], 0.0), consts_pool)
            in_turn(4, pool.affine_select(out=ident_bf[:, :], in_=ident_bf[:, :], compare_op=ALU.not_equal,
                                          fill=1.0, base=0, pattern=[[-1, P]], channel_multiplier=1), consts_pool)
            in_turn(5, pool.memset(causal[:, :], 0.0), consts_pool)
            in_turn(6, pool.affine_select(out=causal[:, :], in_=causal[:, :], compare_op=ALU.is_ge, fill=MASKED,
                                          base=0, pattern=[[-1, P]], channel_multiplier=1), consts_pool)
            in_turn(7, pool.memset(all_masked[:, :], MASKED), consts_pool)
            in_turn(8, pool.memset(f32(decay[:, :]), 0.0), consts_pool)
            in_turn(9, pool.memset(pick[:, :], 0.0), consts_pool)
            for k in range(P // 32):
                in_turn(10 + k, pool.affine_select(out=pick[:, :], in_=pick[:, :], compare_op=ALU.not_equal,
                                                   fill=1.0, base=-32 * k, pattern=[[-1, HEADS]],
                                                   channel_multiplier=1), consts_pool)
            in_turn(1, pool.memset(half[:, :], -0.5), consts)

            def pow_rstd(nn):
                pool.wait_ge(ms_ready, nn + 1)
                in_turn(nn + 1, pool.tensor_tensor(rstd[:, :], ms[:, :], half[:, :], ALU.pow), rstd_ready)

            def fox_picks():
                pool.wait_ge(unit_used, FOX_BASE)
                for t in range(HEADS):
                    par, j = t % 2, t // 2
                    if par == 0 and j >= 1:
                        pool.wait_ge(scored, TB * (t - 1))
                    if par == 1 and j >= 2:
                        pool.wait_ge(scored, TB * (t - 3))
                    rows, at = beside(par), FOX_Q_AT[par][j % 2]
                    in_turn(t + 1, pool.tensor_copy(wide_lo[rows, at:at + SEQ],
                                                    pick[rows, t:t + 1].to_broadcast([64, SEQ])), picked)

            def zero_window_half():
                pool.wait_ge(unit_used, SWA_BASE)
                in_turn(1, pool.memset(f32(wide_lo[64:128, Q_AT:Q_AT + 2 * CHUNKS * P]), 0.0), zeroed)

            pow_rstd(0)
            pow_rstd(1)
            fox_picks()
            pow_rstd(2)
            pow_rstd(3)
            zero_window_half()
            pow_rstd(4)
            pow_rstd(5)
            pow_rstd(6)

        @block.tensor
        def _(pe):
            def products(out, pairs, first, last):
                n = 3 * len(pairs)
                k = 0
                for (a_hi, a_lo), (b_hi, b_lo) in pairs:
                    for a, b in ((a_hi, b_hi), (a_hi, b_lo), (a_lo, b_hi)):
                        mm = pe.matmul(out, a, b, start=first and k == 0, stop=last and k == n - 1)
                        k += 1
                return mm

            def w(slot, a, b):
                return w_hi[:, slot, a:b], w_lo[:, slot, a:b]

            def u(kb):
                return blk(u_hi, kb), blk(u_lo, kb)

            def u_tokens(kb, t):
                a = kb * SEQ + t * P
                return u_hi[:, a:a + P], u_lo[:, a:a + P]

            def wide(a, b):
                return wide_hi[:, a:b], wide_lo[:, a:b]

            def token_sums(nn, b):
                pe.wait_ge(acc_ready, 9 * nn + 9)
                for t in range(TB):
                    mm = pe.matmul(bank[b][:, 2 * t:2 * t + 2], acc[:, t * P:(t + 1) * P], ones[:, 0:2],
                                   start=True, stop=True)
                mm.then_inc(tok_sum, 1)

            def row_sums(nn):
                pe.wait_ge(diag_ready, nn + 1)
                pe.matmul(bank[5][:, :], ones[:, :], diag[:, :], start=True, stop=True).then_inc(row_sum, 1)

            def turn_x(m):
                if m % 2 == 0:
                    pe.wait_ge(x_loaded[m // 2], 16)
                if m >= 4:
                    pe.wait_ge(h_ready, m - 3)
                for t in range(TB):
                    mm = pe.transpose(bank[4 + m % 4][:, t * P:(t + 1) * P],
                                      x_piece(m // 2)[:, t, m % 2 * P:(m % 2 + 1) * P], ident[:, :])
                mm.then_inc(x_turned, 1)

            pe.wait_ge(ident_ready, 1)
            for m in range(4):
                turn_x(m)

            def ffn(f, nn):
                base = FFN_BASE[f]

                def in_body(i):
                    peeled = type(i) is int
                    for r in range(IN_UNITS):
                        slot = (base + r) % SPLIT
                        pe.wait_ge(w_ready, base + 4 * i + r + 1)
                        if not peeled and r == 0:
                            pe.wait_ge(gate_scaled, FB * f + 2 * i)
                        if not peeled and r == 2:
                            pe.wait_ge(up_scaled, FB * f + 2 * i)
                        for q in range(4):
                            kb = 4 * (r % 2) + q
                            if peeled and r < 2:
                                if f == 0 and kb in (2, 4):
                                    turn_x(kb + 2)
                                    turn_x(kb + 3)
                                pe.wait_ge(u_ready, 8 * nn + kb + 1)
                            for c in range(2):
                                a = q * 256 + c * P
                                mm = products(bank[2 * (r // 2) + c][:, :], [(w(slot, a, a + P), u(kb))],
                                              kb == 0, kb == KB - 1)
                            if f == 0 and peeled and r == 2 and q == 2:
                                token_sums(nn, 5)
                        mm.then_inc(unit_used, 1)
                        if f > 0 and peeled and r == 1:
                            token_sums(nn, 5)
                        if peeled and r == 2:
                            row_sums(nn)

                in_body(0)
                with pe.Fori(1, IN_BODIES) as i:
                    in_body(i)
                pe.wait_ge(a_ready, FB * (f + 1) - 4)
                out_stage(base + IN_BODIES * IN_UNITS, nn + 1, OUT_KBS, 0, final_wait=FB * (f + 1))

            def out_pair(n, m, ready, per_pair):
                for k, kbs in enumerate(WO_KBS):
                    at = n + len(WO_KBS) * m + k
                    for q, kb in enumerate(kbs):
                        if q == 0:
                            pe.wait_ge(w_ready, at + 1)
                        if m < 2:
                            pe.wait_ge(ready, per_pair * (kb + 1))
                        for c in range(2):
                            a = q * 256 + c * P
                            o_at = O_AT + kb * SEQ
                            mm = products(bank[2 * m + c][:, :], [(w(at % SPLIT, a, a + P), wide(o_at, o_at + SEQ))],
                                          kb == 0, kb == KB - 1)
                        if q == len(kbs) - 1:
                            mm.then_inc(unit_used, 1)
                        yield

            def first_out_pairs(n, order, free, ready, per_pair, scores_read):
                pair_0, pair_1 = (out_pair(n, m, ready, per_pair) for m in range(2))
                pe.wait_ge(*free)
                for k, m in enumerate(order):
                    if m and 1 not in order[:k]:
                        pe.wait_ge(*scores_read)
                    next(pair_1 if m else pair_0)
                    yield
                next(pair_1)
                for _ in pair_0:
                    pass
                for _ in pair_1:
                    pass

            def mixer_out_stage(n, nn, fill, ready, per_pair):
                for _ in fill:
                    pass
                pe.wait_ge(h_ready, 8 * nn)
                for m in range(2, KB // 2):
                    for _ in out_pair(n, m, ready, per_pair):
                        pass

            def out_stage(base, nn, kbs, at, final_wait=None):
                units = 2 * len(kbs)

                def body(i):
                    for r in range(units):
                        mp, k = divmod(r, len(kbs))
                        slot = (base + r) % SPLIT
                        pe.wait_ge(w_ready, base + units * i + r + 1)
                        if k == 0:
                            pe.wait_ge(h_ready, 8 * nn + 4 * i + 2 * mp - 2)
                        if final_wait is not None:
                            if r == len(kbs) - 2:
                                pe.wait_ge(a_ready, final_wait)
                        for q, kb in enumerate(kbs[k]):
                            for c in range(2):
                                a = q * 256 + c * P
                                mm = products(bank[4 + 2 * mp + c][:, :],
                                              [(w(slot, a, a + P), wide(at + kb * SEQ, at + (kb + 1) * SEQ))],
                                              kb == 0, kb == kbs[-1][-1])
                        mm.then_inc(unit_used, 1)

                with pe.Fori(0, OUT_BODIES) as i:
                    body(i)

            def project(n, b, free_at):
                for kb in range(KB):
                    if kb == 0:
                        pe.wait_ge(w_ready, n + 1)
                        if free_at is not None:
                            pe.wait_ge(*free_at)
                    mm = products(bank[b][:, :], [(w(n % SPLIT, kb * P, (kb + 1) * P), u(kb))],
                                  kb == 0, kb == KB - 1)
                    if kb == KB - 1:
                        mm.then_inc(unit_used, 1)
                    yield

            def fox(nn):
                n = FOX_BASE
                for k in range(V_UNITS):
                    pe.wait_ge(w_ready, n + 1)
                    if k == 0:
                        pe.wait_ge(u_ready, 8 * nn + 2)
                    if k == V_UNITS // 2:
                        pe.wait_ge(row_ready, nn + 1)
                        pe.wait_ge(f_chain, 1)
                    for t in range(TB):
                        for q in range(2):
                            kb = 2 * (k % 4) + q
                            mm = products(bank[4 * (k // 4) + t][:, :],
                                          [(u_tokens(kb, t), w(n % SPLIT, q * 512, (q + 1) * 512))],
                                          kb == 0, kb == KB - 1)
                    mm.then_inc(unit_used, 1)
                    n += 1
                    if k == 0:
                        pe.wait_ge(w_ready, n + 1)
                        for kb in range(KB):
                            pe.wait_ge(u_ready, 8 * nn + kb + 1)
                            mm = products(bank[4][0:HEADS, :], [(w(n % SPLIT, kb * HEADS, (kb + 1) * HEADS), u(kb))],
                                          kb == 0, kb == KB - 1)
                        mm.then_inc(unit_used, 1)
                        n += 1
                        token_sums(nn, 5)
                    if k == 1:
                        row_sums(nn)

                def score(t, i):
                    par, j = t % 2, t // 2
                    q_at = FOX_Q_AT[par][j % 2] + i * P
                    k_at = FOX_K_AT[par]
                    nk = FOX_KEYS[i]
                    out = bank[FOX_BANK[i]][:, FOX_BANK_AT[i]:FOX_BANK_AT[i] + nk]
                    for k, part in enumerate((wide_hi, wide_lo)):
                        pe.matmul(out, part[:, q_at:q_at + P], part[:, k_at:k_at + nk], start=k == 0, stop=False)
                    pe.matmul(out[:, nk - P:nk], ident_bf[:, :], causal[:, :],
                              start=False, stop=True).then_inc(scored, 1)

                def turn(t, kb):
                    at = TB * t + kb
                    if kb == 0:
                        pe.wait_ge(p_ready, t + 1)
                    if at >= 2:
                        pe.wait_ge(pt_ready, at - 1)
                    for k, i in enumerate(range(kb, TB)):
                        a = FOX_P_AT[i] + kb * P
                        mm = pe.transpose(bank[5 + at % 2][:, k * P:(k + 1) * P], prob[t % 2][:, a:a + P],
                                          ident[:, :])
                    mm.then_inc(turned, 1)

                def value(t, kb):
                    at = TB * t + kb
                    pe.wait_ge(pt_ready, at + 1)
                    if kb == 0 and t:
                        pe.wait_ge(o_ready, t)
                    v_at = V_AT + kb * D + t * DH
                    p_at = PT_AT + (at % 2) * SEQ
                    cols = SEQ - kb * P
                    products(bank[7][0:DH, kb * P:SEQ],
                             [(wide(v_at, v_at + DH), wide(p_at, p_at + cols))], kb == 0, kb == TB - 1)\
                        .then_inc(pv_done, 1)

                def fillers(n):
                    for m in range(2 * PAIRS):
                        yield from project(n + m, m % 2, (qk_scaled, m - 1) if m >= 2 else None)
                    yield from first_out_pairs(n + 2 * PAIRS, [0] * 7 + [1], (qk_scaled, 2 * PAIRS), o_ready, 2,
                                               (expd, TB * HEADS))

                fill = fillers(n)
                n += 2 * PAIRS + len(WO_KBS)
                AHEAD = 3
                pe.wait_ge(v_ready, TB)
                for _ in range(2 * KB + AHEAD):
                    next(fill)
                for t in range(HEADS + 1):
                    j = t // 2
                    steps = ["f", "f"]
                    if t < HEADS:
                        steps += [("s", 3), "f", ("s", 2), "f"]
                    if t:
                        steps += [("t", 0), "f"]
                    if t < HEADS:
                        steps += [("s", 0), ("s", 1)]
                    if t:
                        steps += [("t", 1), "f", ("v", 0), ("t", 2), "f", ("v", 1), ("t", 3), "f", ("v", 2)]
                    steps += ["f"] * (KB - steps.count("f"))
                    if t:
                        steps += [("v", 3)]
                    allowed = {HEADS - 3: range(KB - AHEAD), HEADS - 2: (0, 3, 6), HEADS - 1: (0, 3, 6),
                               HEADS: (0, 4)}.get(t, range(KB))
                    fillers = 0
                    for s in steps:
                        if s == "f":
                            if fillers in allowed:
                                next(fill, None)
                            fillers += 1
                        elif s[0] == "s":
                            if s[1] == 3:
                                if t == 0:
                                    pe.wait_ge(decay_placed, 1)
                                    pe.wait_ge(v_ready, 2 * TB)
                                pe.wait_ge(picked, t + 1)
                                pe.wait_ge(qk_copied, 2 * j + 2)
                                pe.wait_ge(qk_ready, 2 * j + 2)
                            if t:
                                pe.wait_ge(expd, TB * t)
                            score(t, s[1])
                        elif s[0] == "t":
                            turn(t - 1, s[1])
                        else:
                            value(t - 1, s[1])
                mixer_out_stage(n - len(WO_KBS), nn + 1, fill, o_ready, 2)

            def window(nn):
                n = SWA_BASE
                k_steps, v_steps = project(n, 1, None), project(n + 1, 2, None)
                n += 2
                for steps, first, last in ((k_steps, 0, 6), (v_steps, 0, 6), (k_steps, 6, 8), (v_steps, 6, 8)):
                    for kb in range(first, last):
                        pe.wait_ge(u_ready, 8 * nn + kb + 1)
                        if kb < KB - 1:
                            next(steps)
                        else:
                            for _ in steps:
                                pass
                token_sums(nn, 5)

                def score(j, half):
                    if j:
                        pe.wait_ge(w_expd, CHUNKS * (j - 1) + HALF * (half + 1))
                    for n in range(HALF * half, HALF * (half + 1)):
                        out = bank[2 + half][:, (n % HALF) * P:(n % HALF + 1) * P]
                        k_at = K_AT + j // GROUP_PAIRS * SEQ + max(0, n - 1) * CHUNK
                        q_at = Q_AT + ((j % 2) * CHUNKS + n) * P
                        for k, part in enumerate((wide_hi, wide_lo)):
                            mm = pe.matmul(out, part[:, q_at:q_at + P], wide_hi[:, k_at:k_at + P],
                                           start=k == 0, stop=k == 1 and n > 0)
                        if n == 0:
                            mm = pe.matmul(out[:, CHUNK:P], ident_bf[:, :], all_masked[:, :],
                                           start=False, stop=True)
                    mm.then_inc(w_scored, 1)

                def turn(j, half):
                    pe.wait_ge(w_p_ready, j + 1)
                    if j:
                        pe.wait_ge(w_pt_ready, 2 * (j - 1) + half + 1)
                    for k in range(HALF):
                        a = (HALF * half + k) * P
                        mm = pe.transpose(bank[4 + half][:, k * P:(k + 1) * P], wprob[j % 2][:, a:a + P], ident[:, :])
                    mm.then_inc(w_turned, 1)

                def value(j, half):
                    pe.wait_ge(w_pt_ready, 2 * j + half + 1)
                    if j == 0:
                        pe.wait_ge(v_moved, 1)
                    if j:
                        pe.wait_ge(w_o_ready, 2 * (j - 1) + half + 1)
                    for n in range(HALF * half, HALF * (half + 1)):
                        v_at = V_AT + n // 2 * P if n % 2 or n == 0 else VS_AT + (n // 2 - 1) * P
                        v_at += j // GROUP_PAIRS * DH
                        p_at = PT_AT + half * SEQ + (n % HALF) * P
                        mm = products(bank[6 + half][0:DH, (n % HALF) * P:(n % HALF + 1) * P],
                                      [(wide(v_at, v_at + DH), wide(p_at, p_at + P))], True, True)
                    mm.then_inc(w_pv_done, 1)

                def fillers(n):
                    for j in range(PAIRS):
                        free_at = (w_q_scaled, j - 1) if j > 1 else (w_k_scaled, 1) if j else None
                        yield from project(n + j, j % 2, free_at)
                    yield from first_out_pairs(n + PAIRS, [0] * 6 + [1, 0], (w_q_scaled, PAIRS), w_o_ready, 2,
                                               (w_expd, CHUNKS * PAIRS))

                fill = fillers(n)
                n += PAIRS + len(WO_KBS)

                def f(steps):
                    for _ in range(steps):
                        next(fill, None)

                f(5)
                row_sums(nn)
                f(KB + 2)
                for j in range(PAIRS + 1):
                    before, after_0, after_1, between, end = {PAIRS - 2: (1, 0, 0, 1, 2), PAIRS - 1: (1, 1, 0, 0, 1),
                                                              PAIRS: (0, 0, 1, 1, 0)}.get(j, (1, 0, 3, 2, 2))
                    f(before)
                    if j < PAIRS:
                        if j == 0:
                            pe.wait_ge(zeroed, 1)
                        if j % GROUP_PAIRS == 0:
                            pe.wait_ge(w_k_ready, j // GROUP_PAIRS + 1)
                        pe.wait_ge(w_q_copied, j + 1)
                        pe.wait_ge(w_q_ready, j + 1)
                        score(j, 0)
                    if j == 0:
                        pe.wait_ge(w_v_biased, 1)
                        for t in range(TB):
                            mm = pe.transpose(bank[7][:, t * P:(t + 1) * P], sq[:, 0, t * P:(t + 1) * P], ident[:, :])
                        mm.then_inc(w_v_turned, 1)
                    f(after_0)
                    if j:
                        turn(j - 1, 0)
                    if j < PAIRS:
                        score(j, 1)
                    f(after_1)
                    if j:
                        turn(j - 1, 1)
                        value(j - 1, 0)
                    f(between)
                    if j:
                        value(j - 1, 1)
                    f(end)
                mixer_out_stage(n - len(WO_KBS), nn + 1, fill, w_o_ready, 2)

            ffn(0, 0)
            fox(1)
            ffn(1, 2)
            ffn(2, 3)
            window(4)
            ffn(3, 5)
            for half_d in range(2):
                for t in range(TB):
                    if half_d == 1 and t == TB - 1:
                        pe.wait_ge(ms_ready, 7)
                    for k in range(4):
                        m = 4 * half_d + k
                        if t == 0:
                            pe.wait_ge(u_hi_ready, 8 * 6 + m + 1)
                        if t == 0 and half_d == 1 and k == 3:
                            token_sums(6, 7)
                        mm = pe.transpose(bank[4 * half_d + t][:, k * P:(k + 1) * P],
                                          h[:, m * SEQ + t * P:m * SEQ + (t + 1) * P], ident[:, :])
                    mm.then_inc(y_turned, 1)

        @block.scalar
        def _(act):
            act.dma_start(gain[:, :], gains).then_inc(gain_loaded, 16)

            def split_hi(r, base, cols, count):
                act.wait_ge(raw_loaded[(base + r) % RAW], count)
                slot = (base + r) % SPLIT
                act.activation(w_hi[:, slot, 0:cols], raw[:, (base + r) % RAW, 0:cols], ACT.Copy)\
                   .then_inc(w_hi_ready, 1)

            def split_next(used, base, r, turn_of, cols=UNIT):
                act.wait_ge(unit_used, used)
                q = r + LOOK
                split_hi(q, base, cols, 16 * (turn_of + (base + q) // RAW + 1))

            def scaled_block(nn, i4, r):
                m_at = (i4 + r) * SEQ
                if nn == 6:
                    act.wait_ge(sq_ready, 8 * nn + i4 + r + 1)
                act.wait_ge(h_ready, 8 * nn + i4 + r + 1)
                act.activation(dyn(u_hi if nn < 6 else h, m_at), dyn(h, m_at), ACT.Copy,
                               scale=gain[:, bass.ds(8 * nn + i4 + r, 1)]).then_inc(u_hi_ready, 1)

            def square(i4, r):
                act.activation(sq[:, r % 2, :], dyn(h, (i4 + r) * SEQ), ACT.Square).then_inc(sq_ready, 1)

            def post_pair(nn, i4, r):
                for c in range(2):
                    act.wait_ge(acc_ready, 9 * nn + i4 + r + c)
                    if nn < 6:
                        scaled_block(nn, i4, r + c)
                    else:
                        act.wait_ge(h_ready, 8 * nn + i4 + r + c + 1)
                    square(i4, r + c)
                if nn == 6:
                    for c in range(2):
                        scaled_block(nn, i4, r + c)

            split_hi(0, 0, UNIT, 16)
            act.wait_ge(gain_loaded, 16)
            for m in range(KB):
                scaled_block(0, 0, m)
                if m == 3:
                    split_hi(1, 0, UNIT, 16)

            def row_copy(nn):
                act.wait_ge(row_sum, nn + 1)
                act.activation(rstd_row[:, :], bank[5][:, :], ACT.Copy).then_inc(row_ready, 1)

            def ffn(f, nn, last):
                base = FFN_BASE[f]

                def in_body(i):
                    for r in range(IN_UNITS):
                        split_next(base + 4 * i + r + 1, base, r, i)
                        if f == 0 and type(i) is int and r == 0:
                            for m in range(KB):
                                act.wait_ge(acc_ready, m)
                                square(0, m)
                        if type(i) is int and r == 2:
                            row_copy(nn)
                        if r == 2:
                            for c in range(2):
                                act.wait_ge(gate_scaled, FB * f + 2 * i + c + 1)
                                act.activation(silu_buf[:, c * SEQ:(c + 1) * SEQ],
                                               g_scaled_buf[:, c * SEQ:(c + 1) * SEQ], ACT.Silu)\
                                   .then_inc(silu_ready, 1)
                        if r == 3:
                            for c in range(2):
                                act.wait_ge(prod_ready, FB * f + 2 * i + c + 1)
                                act.activation(dyn(wide_hi, 2 * SEQ * i + c * SEQ),
                                               up_buf[:, c * SEQ:(c + 1) * SEQ], ACT.Copy)\
                                   .then_inc(a_hi_ready, 1)

                in_body(0)
                with act.Fori(1, IN_BODIES) as i:
                    in_body(i)
                out_stage(base + IN_BODIES * IN_UNITS, nn + 1, OUT_KBS, OUT_COLS, last)

            def out_stage(base, nn, kbs, cols, last=False, first_split=False):
                units = 2 * len(kbs)

                def body(i):
                    for r in range(units):
                        if first_split and i == 0 and r == 0:
                            continue
                        if not (last and type(i) is int and i == OUT_BODIES - 1 and r + LOOK >= units):
                            split_next(base + units * i + r + 1, base, r, units // RAW * i,
                                       cols if r + LOOK < units else UNIT)
                        if r % len(kbs) == len(kbs) - 1:
                            post_pair(nn, 4 * i, 2 * (r // len(kbs)))

                if last or first_split:
                    for i in range(OUT_BODIES):
                        body(i)
                else:
                    with act.Fori(0, OUT_BODIES) as i:
                        body(i)

            def step(n):
                split_next(n + 1, n, 0, 0)

            def project_hi(count, j, is_q):
                act.wait_ge(qk_scaled, count)
                for par in range(2):
                    own = slice(64 * par, 64 * par + 64)
                    at = FOX_Q_AT[par][j % 2] if is_q else FOX_K_AT[par]
                    last = act.activation(wide_hi[own, at:at + SEQ], scaled[own, :], ACT.Copy)
                last.then_inc(qk_hi_ready, 1)

            def project_copy(j, is_q):
                for par in range(2):
                    own = slice(64 * par, 64 * par + 64)
                    at = FOX_Q_AT[par][j % 2] if is_q else FOX_K_AT[par]
                    to = wide_hi[beside(par), at:at + SEQ] if is_q else wide_lo[own, at:at + SEQ]
                    last = act.activation(to, scaled[own, :], ACT.Copy)
                last.then_inc(qk_copied, 1)

            def fox(nn):
                n = FOX_BASE
                step(n)
                n += 1
                step(n)
                n += 1
                row_copy(nn)
                for k in range(1, V_UNITS):
                    step(n)
                    n += 1
                    if k == 1:
                        act.wait_ge(consts, 1)
                        act.wait_ge(f_chain, 3)
                        act.activation(scratch[0:HEADS, 512:1024], scratch[0:HEADS, 512:1024], ACT.Exp, scale=-1.0)\
                           .then_inc(f_act, 1)
                        act.wait_ge(f_act, 1)
                        act.activation(scratch[0:HEADS, 512:1024], scratch[0:HEADS, 512:1024], ACT.Ln,
                                       bias=ones[0:HEADS, 0:1]).then_inc(f_act, 1)
                    if k == 2:
                        act.wait_ge(f_chain, 7)
                        act.activation(decay[0:HEADS, :], scratch[0:HEADS, 0:512], ACT.Copy)\
                           .then_inc(f_act, 1)
                    if k % 4 == 3:
                        for t in range(TB):
                            act.wait_ge(rstd_ready, nn + 1)
                            a = V_AT + t * D + (k // 4) * 512
                            act.activation(wide_hi[:, a:a + 512], bank[4 * (k // 4) + t][:, :], ACT.Copy,
                                           scale=rstd[:, t:t + 1]).then_inc(v_hi_ready, 1)
                act.wait_ge(decay_ready, 1)
                for par in range(2):
                    last = act.activation(wide_lo[beside(par), FOX_K_AT[par]:FOX_K_AT[par] + SEQ],
                                          f32(decay[0:64, :]), ACT.Copy)
                last.then_inc(decay_placed, 1)
                for k in range(2):
                    step(n)
                    n += 1
                    project_hi(k + 1, 0, k == 0)
                    project_copy(0, k == 0)

                for t in range(HEADS + 1):
                    j = t // 2
                    b = t % 2

                    def pt_hi(kb):
                        at = TB * (t - 1) + kb
                        cols = SEQ - kb * P
                        act.wait_ge(turned, at + 1)
                        if at >= 2:
                            act.wait_ge(pv_done, at - 1)
                        a = PT_AT + (at % 2) * SEQ
                        act.activation(wide_hi[:, a:a + cols], bank[5 + at % 2][:, 0:cols], ACT.Copy)\
                           .then_inc(pt_hi_ready, 1)

                    def exp(i):
                        nk = FOX_KEYS[i]
                        act.wait_ge(nmax_ready, TB * t + (TB if i < 2 else ORDER.index(i) + 1))
                        act.activation(prob[b][:, FOX_P_AT[i]:FOX_P_AT[i] + nk],
                                       bank[FOX_BANK[i]][:, FOX_BANK_AT[i]:FOX_BANK_AT[i] + nk], ACT.Exp,
                                       bias=nmax[:, b, i:i + 1], accum_out=psum_p[:, b, i:i + 1])\
                           .then_inc(expd, 1)

                    if t:
                        pt_hi(0)
                    if t < HEADS:
                        if t >= 2:
                            act.wait_ge(turned, TB * (t - 1))
                            act.wait_ge(rsum_ready, t - 1)
                        exp(3)
                        exp(2)
                    if t:
                        pt_hi(1)
                    if t < HEADS:
                        exp(0)
                        exp(1)
                    if j + 1 < PAIRS:
                        act.wait_ge(scored, TB * (t + 1))
                        project_hi(t + 3, j + 1, b == 0)
                    if t:
                        pt_hi(2)
                        pt_hi(3)
                    if j + 1 < PAIRS:
                        project_copy(j + 1, b == 0)
                    if t:
                        par, jo = (t - 1) % 2, (t - 1) // 2
                        act.wait_ge(pv_done, TB * t)
                        act.activation(wide_hi[64 * par:64 * par + 64, O_AT + jo * SEQ:O_AT + (jo + 1) * SEQ],
                                       bank[7][0:DH, :], ACT.Copy).then_inc(o_hi_ready, 1)
                    if j + 1 < PAIRS or t == HEADS - 1:
                        step(n)
                        n += 1
                out_stage(n - 1, nn + 1, WO_KBS, UNIT, first_split=True)

            def window_q_hi(j):
                act.wait_ge(w_q_scaled, j + 1)
                for par in range(2):
                    own = slice(64 * par, 64 * par + 64)
                    last = act.activation(window_q(wide_hi, par, par, j), chunks(scaled[own, :]), ACT.Identity,
                                          bias=bq_scaled[own, j:j + 1])
                last.then_inc(w_q_hi_ready, 1)

            def window_q_copy(j):
                for par in range(2):
                    own = slice(64 * par, 64 * par + 64)
                    last = act.activation(window_q(wide_hi, 1 - par, par, j), chunks(scaled[own, :]), ACT.Identity,
                                          bias=bq_scaled[own, j:j + 1])
                last.then_inc(w_q_copied, 1)

            def window_k_hi(g):
                act.wait_ge(w_k_scaled, 1)
                own, a = slice(64 * g, 64 * g + 64), K_AT + g * SEQ
                last = act.activation(wide_hi[0:64, a:a + SEQ], sq[own, 1, :], ACT.Identity, bias=bk[own, :])
                if g:
                    last = act.activation(wide_lo[own, a:a + SEQ], sq[own, 1, :], ACT.Identity, bias=bk[own, :])
                last.then_inc(w_k_hi_ready, 1)

            def window_v_hi():
                act.wait_ge(w_v_turned, 1)
                act.activation(wide_hi[:, V_AT:V_AT + SEQ], bank[7][:, :], ACT.Copy).then_inc(w_v_hi_ready, 1)
                act.wait_ge(w_v_hi_ready, 1)
                act.activation(wide_hi[0:64, VS_AT:VS_AT + 3 * P], f32(wide_hi[64:128, V_AT:V_AT + 3 * P]), ACT.Copy)
                act.activation(wide_hi[64:128, VS_AT:VS_AT + 3 * P], f32(wide_hi[0:64, V_AT + P:V_AT + 4 * P]),
                               ACT.Copy).then_inc(v_moved_hi, 1)

            def window(nn):
                n = SWA_BASE
                for _ in range(2):
                    step(n)
                    n += 1
                act.wait_ge(biases_ready, 1)
                row_copy(nn)
                window_k_hi(0)
                window_q_hi(0)
                window_q_copy(0)
                step(n)
                n += 1

                for j in range(PAIRS + 1):
                    b = j % 2

                    def exps(half):
                        act.wait_ge(w_nmax_ready, 2 * j + half + 1)
                        if half == 0 and j >= 2:
                            act.wait_ge(w_turned, 2 * (j - 1))
                            act.wait_ge(w_rsum_ready, j - 1)
                        for c in range(HALF * half, HALF * (half + 1)):
                            act.activation(wprob[b][:, c * P:(c + 1) * P],
                                           bank[2 + half][:, (c % HALF) * P:(c % HALF + 1) * P], ACT.Exp,
                                           bias=wmax[:, b, c:c + 1], accum_out=wsum[:, b, c:c + 1])\
                               .then_inc(w_expd, 1)

                    def pt_hi(half):
                        act.wait_ge(w_turned, 2 * (j - 1) + half + 1)
                        if j >= 2:
                            act.wait_ge(w_pv_done, 2 * (j - 2) + half + 1)
                        a = PT_AT + half * SEQ
                        act.activation(wide_hi[:, a:a + SEQ], bank[4 + half][:, :], ACT.Copy)\
                           .then_inc(w_pt_hi_ready, 1)

                    def o_hi(j, half):
                        act.wait_ge(w_pv_done, 2 * j + half + 1)
                        a = O_AT + j * SEQ + half * HALF * CHUNK
                        for par in range(2):
                            last = act.activation(chunks(wide_hi[64 * par:64 * par + 64, a:a + HALF * CHUNK]),
                                                  pair_output(bank[6 + half], par), ACT.Copy)
                        last.then_inc(w_o_hi_ready, 1)

                    if j >= 2:
                        o_hi(j - 2, 1)
                    if j:
                        pt_hi(0)
                    if j < PAIRS:
                        exps(0)
                    if j:
                        pt_hi(1)
                    if j + 1 < PAIRS:
                        if j:
                            act.wait_ge(w_scored, 2 * j)
                        window_q_hi(j + 1)
                    if j < PAIRS:
                        exps(1)
                        act.activation(esink[:, b, :], wmax[:, b, :], ACT.Exp, bias=sink[:, j:j + 1])\
                           .then_inc(w_esink_ready, 1)
                    if j + 1 < PAIRS:
                        window_q_copy(j + 1)
                    if j < PAIRS:
                        step(n)
                        n += 1
                    if j:
                        o_hi(j - 1, 0)
                    if j == 0:
                        window_v_hi()
                    if j == 2:
                        window_k_hi(1)
                o_hi(PAIRS - 1, 1)
                out_stage(n - 1, nn + 1, WO_KBS, UNIT, first_split=True)

            ffn(0, 0, False)
            fox(1)
            ffn(1, 2, False)
            ffn(2, 3, False)
            window(4)
            ffn(3, 5, True)
            act.wait_ge(rstd_ready, 7)
            for n in range(1, 2 * TB, 2):
                t = n % TB
                act.wait_ge(y_turned, n + 1)
                act.activation(raw[:, n // 2, (n % 2) * 512:(n % 2 + 1) * 512], bank[n][:, :], ACT.Copy,
                               scale=rstd[:, t:t + 1]).then_inc(y_scaled_act, 1)

        @block.vector
        def _(dve):
            def split_lo(n_mod, count, cols=UNIT):
                dve.wait_ge(w_hi_ready, count)
                s, r = n_mod % SPLIT, n_mod % RAW
                dve.tensor_tensor(w_lo[:, s, 0:cols], raw[:, r, 0:cols], f32(w_hi[:, s, 0:cols]),
                                  ALU.subtract).then_inc(w_ready, 1)

            def residual(i4, r, src, scale):
                m_at = (i4 + r) * SEQ
                dve.scalar_tensor_tensor(out=dyn(h, m_at), in0=src, scalar=scale, in1=dyn(h, m_at),
                                         op0=ALU.mult, op1=ALU.add).then_inc(h_ready, 1)

            def scaled_lo(nn, i4, r):
                m_at = (i4 + r) * SEQ
                dve.wait_ge(u_hi_ready, 8 * nn + i4 + r + 1)
                dve.scalar_tensor_tensor(out=dyn(u_lo, m_at), in0=dyn(h, m_at),
                                         scalar=gain[:, bass.ds(8 * nn + i4 + r, 1)],
                                         in1=f32(dyn(u_hi, m_at)), op0=ALU.mult, op1=ALU.subtract)\
                   .then_inc(u_ready, 1)

            def add_squares(nn, i4, r):
                dve.wait_ge(sq_ready, 8 * nn + i4 + r + 1)
                dve.wait_ge(acc_ready, 9 * nn + i4 + r + 1)
                dve.tensor_tensor(acc[:, :], acc[:, :], sq[:, r % 2, :], ALU.add).then_inc(acc_ready, 1)

            def mean_squares(nn, b):
                dve.wait_ge(tok_sum, nn + 1)
                dve.tensor_scalar(ms[:, :], bank[b][:, 0:2 * TB].rearrange("p (t two) -> p t two", two=2)[:, :, 0],
                                  1.0 / D, RMS_EPS, ALU.mult, ALU.add).then_inc(ms_ready, 1)
                if nn < 6:
                    dve.memset(acc[:, :], 0.0).then_inc(acc_ready, 1)

            def diagonals(nn):
                dve.wait_ge(rstd_ready, nn + 1)
                for t in range(TB):
                    last = dve.tensor_scalar(diag[:, t * P:(t + 1) * P], ident[:, :], rstd[:, t:t + 1], None,
                                             ALU.mult)
                last.then_inc(diag_ready, 1)

            dve.memset(acc[:, :], 0.0).then_inc(acc_ready, 1)
            split_lo(0, 1)
            for g in range(KB // 2):
                for m in (2 * g, 2 * g + 1):
                    dve.wait_ge(x_turned, m + 1)
                    dve.tensor_copy(h[:, m * SEQ:(m + 1) * SEQ], bank[4 + m % 4][:, :]).then_inc(h_ready, 1)
                if g == 0:
                    dve.wait_ge(gain_loaded, 16)
                for m in (2 * g, 2 * g + 1):
                    scaled_lo(0, 0, m)
                if g == 1:
                    split_lo(1, 2)
            dve.wait_ge(consts, 1)

            def ffn(f, nn, last):
                base = FFN_BASE[f]

                def in_body(i):
                    first = type(i) is int
                    for r in range(IN_UNITS):
                        split_lo(base + r + LOOK, base + 4 * i + r + LOOK + 1)
                        if f == 0 and first and r == 0:
                            for m in range(KB):
                                add_squares(0, 0, m)
                        if f == 0 and first and r == 3:
                            dve.wait_ge(small_loaded, 16 * 6)
                            dve.tensor_scalar(nsink[:, :], sink[:, :], -1.0, None, ALU.mult)
                            dve.tensor_scalar(bq_scaled[:, :], bq[:, :], QSCALE, None, ALU.mult)\
                               .then_inc(biases_ready, 1)
                        if first and r == 1:
                            mean_squares(nn, 5)
                            diagonals(nn)
                        if r == (2 if first else 1):
                            dve.wait_ge(unit_used, base + 4 * i + 2)
                            if first:
                                dve.wait_ge(row_ready, nn + 1)
                            for c in range(2):
                                dve.tensor_tensor(g_scaled_buf[:, c * SEQ:(c + 1) * SEQ], bank[c][:, :],
                                                  rstd_row[:, :], ALU.mult).then_inc(gate_scaled, 1)
                        if r == 3:
                            dve.wait_ge(unit_used, base + 4 * i + 4)
                            for c in range(2):
                                dve.tensor_tensor(up_buf[:, c * SEQ:(c + 1) * SEQ], bank[2 + c][:, :],
                                                  rstd_row[:, :], ALU.mult).then_inc(up_scaled, 1)
                            for c in range(2):
                                up = up_buf[:, c * SEQ:(c + 1) * SEQ]
                                dve.wait_ge(silu_ready, FB * f + 2 * i + c + 1)
                                dve.wait_ge(up_scaled, FB * f + 2 * i + c + 1)
                                dve.tensor_tensor(up, up, silu_buf[:, c * SEQ:(c + 1) * SEQ], ALU.mult)\
                                   .then_inc(prod_ready, 1)
                            for c in range(2):
                                dve.wait_ge(a_hi_ready, FB * f + 2 * i + c + 1)
                                dve.tensor_tensor(dyn(wide_lo, 2 * SEQ * i + c * SEQ),
                                                  up_buf[:, c * SEQ:(c + 1) * SEQ],
                                                  f32(dyn(wide_hi, 2 * SEQ * i + c * SEQ)), ALU.subtract)\
                                   .then_inc(a_ready, 1)

                in_body(0)
                with dve.Fori(1, IN_BODIES) as i:
                    in_body(i)
                out_stage(base + IN_BODIES * IN_UNITS, nn + 1, OUT_KBS, 0.5, OUT_COLS, last)

            def out_stage(base, nn, kbs, scale, cols, last=False, first_split=False):
                units = 2 * len(kbs)

                def body(i):
                    for r in range(units):
                        if first_split and i == 0 and r == 0:
                            continue
                        if not (last and type(i) is int and i == OUT_BODIES - 1 and r + LOOK >= units):
                            split_lo(base + r + LOOK, base + units * i + r + LOOK + 1,
                                     cols if r + LOOK < units else UNIT)
                        if r % len(kbs) == len(kbs) - 1:
                            mp = r // len(kbs)
                            dve.wait_ge(unit_used, base + units * i + r + 1)
                            first_bank = 4 * i + 2 * mp if first_split else 4 + 2 * mp
                            for c in range(2):
                                residual(4 * i, 2 * mp + c, bank[first_bank + c][:, :], scale)
                            for c in range(2):
                                if nn < 6:
                                    scaled_lo(nn, 4 * i, 2 * mp + c)
                                add_squares(nn, 4 * i, 2 * mp + c)

                if last or first_split:
                    for i in range(OUT_BODIES):
                        body(i)
                else:
                    with dve.Fori(0, OUT_BODIES) as i:
                        body(i)

            def step(n):
                split_lo(n + LOOK, n + LOOK + 1)

            def fox(nn):
                n = FOX_BASE
                x0, x1, x2, x3 = (scratch[0:HEADS, 512 * k:512 * k + 512] for k in range(4))
                step(n)
                n += 1
                mean_squares(nn, 5)
                step(n)
                n += 1
                diagonals(nn)
                dve.wait_ge(row_ready, nn + 1)
                dve.wait_ge(unit_used, FOX_BASE + 2)
                dve.tensor_tensor(x0, bank[4][0:HEADS, :], rstd_row[0:HEADS, :], ALU.mult).then_inc(f_chain, 1)
                dve.wait_ge(f_chain, 1)
                dve.tensor_scalar(x0, x0, bf[:, 0:1], None, ALU.add).then_inc(f_chain, 1)
                dve.wait_ge(f_chain, 2)
                dve.scalar_tensor_tensor(out=x1, in0=x0, scalar=-1.0, in1=x0, op0=ALU.mult, op1=ALU.max)\
                   .then_inc(f_chain, 1)
                dve.tensor_scalar(x3, x0, 0.0, None, ALU.min).then_inc(f_chain, 1)
                for k in range(1, V_UNITS):
                    step(n)
                    if k == 1:
                        dve.wait_ge(f_act, 2)
                        dve.wait_ge(f_chain, 4)
                        dve.tensor_tensor(x2, x1, x3, ALU.subtract).then_inc(f_chain, 1)
                        dve.wait_ge(f_chain, 5)
                        dve.memset(x3, 1.0).then_inc(f_chain, 1)
                        dve.wait_ge(f_chain, 6)
                        dve.tensor_tensor_scan(x0, x3, x2, 0.0, ALU.mult, ALU.add).then_inc(f_chain, 1)
                    if k == 2:
                        dve.wait_ge(f_act, 3)
                        dve.tensor_tensor(decay[32:32 + HEADS, :], x0, f32(decay[0:HEADS, :]), ALU.subtract)\
                           .then_inc(decay_ready, 1)
                    n += 1
                    if k % 4 == 3:
                        for t in range(TB):
                            dve.wait_ge(v_hi_ready, TB * (k // 4) + t + 1)
                            a = V_AT + t * D + (k // 4) * 512
                            dve.scalar_tensor_tensor(out=wide_lo[:, a:a + 512], in0=bank[4 * (k // 4) + t][:, :],
                                                     scalar=rstd[:, t:t + 1], in1=f32(wide_hi[:, a:a + 512]),
                                                     op0=ALU.mult, op1=ALU.subtract).then_inc(v_ready, 1)

                def project_scaled(n, is_q, count):
                    if count:
                        dve.wait_ge(qk_ready, count)
                        dve.wait_ge(qk_copied, count)
                    dve.wait_ge(unit_used, n + 1)
                    if is_q:
                        dve.scalar_tensor_tensor(out=scaled, in0=bank[0][:, :], scalar=QSCALE, in1=rstd_row[:, :],
                                                 op0=ALU.mult, op1=ALU.mult).then_inc(qk_scaled, 1)
                    else:
                        dve.tensor_tensor(scaled, bank[1][:, :], rstd_row[:, :], ALU.mult).then_inc(qk_scaled, 1)

                def project_lo(count, j, is_q):
                    dve.wait_ge(qk_hi_ready, count)
                    for par in range(2):
                        own = slice(64 * par, 64 * par + 64)
                        at = FOX_Q_AT[par][j % 2] if is_q else FOX_K_AT[par]
                        to = wide_lo[own, at:at + SEQ] if is_q else wide_hi[beside(par), at:at + SEQ]
                        last = dve.tensor_tensor(to, scaled[own, :], f32(wide_hi[own, at:at + SEQ]), ALU.subtract)
                    last.then_inc(qk_ready, 1)

                for k in range(2):
                    step(n)
                    project_scaled(n, k == 0, k)
                    n += 1
                    project_lo(k + 1, 0, k == 0)

                for t in range(HEADS + 1):
                    j = t // 2
                    b = t % 2

                    def pt_lo(kb):
                        at = TB * (t - 1) + kb
                        cols = SEQ - kb * P
                        a = PT_AT + (at % 2) * SEQ
                        dve.wait_ge(pt_hi_ready, at + 1)
                        dve.tensor_tensor(wide_lo[:, a:a + cols], bank[5 + at % 2][:, 0:cols],
                                          f32(wide_hi[:, a:a + cols]), ALU.subtract).then_inc(pt_ready, 1)

                    def row_max(i):
                        dve.wait_ge(scored, TB * t + (TB if i < 2 else ORDER.index(i) + 1))
                        dve.tensor_reduce(nmax[:, b, i:i + 1],
                                          bank[FOX_BANK[i]][:, FOX_BANK_AT[i]:FOX_BANK_AT[i] + FOX_KEYS[i]],
                                          AX_X, ALU.max, negate=True).then_inc(nmax_ready, 1)

                    if t < HEADS:
                        if t >= 2:
                            dve.wait_ge(expd, TB * (t - 1))
                        row_max(3)
                        row_max(2)
                    if t:
                        pt_lo(0)
                    if t < HEADS:
                        row_max(0)
                        row_max(1)
                    if j + 1 < PAIRS:
                        project_scaled(n, b == 0, t + 2)
                    if t:
                        pt_lo(1)
                        pt_lo(2)
                        pt_lo(3)
                    if j + 1 < PAIRS:
                        project_lo(t + 3, j + 1, b == 0)
                    if t < HEADS:
                        dve.wait_ge(expd, TB * (t + 1))
                        dve.reciprocal(rsum[:, b, :], psum_p[:, b, :]).then_inc(rsum_ready, 1)
                        dve.wait_ge(rsum_ready, t + 1)
                        for i in ORDER:
                            part = prob[b][:, FOX_P_AT[i]:FOX_P_AT[i] + FOX_KEYS[i]]
                            last = dve.tensor_scalar(part, part, rsum[:, b, i:i + 1], None, ALU.mult)
                        last.then_inc(p_ready, 1)
                    if t:
                        par, jo = (t - 1) % 2, (t - 1) // 2
                        rows = slice(64 * par, 64 * par + 64)
                        a = O_AT + jo * SEQ
                        dve.wait_ge(o_hi_ready, t)
                        dve.tensor_tensor(wide_lo[rows, a:a + SEQ], bank[7][0:DH, :], f32(wide_hi[rows, a:a + SEQ]),
                                          ALU.subtract).then_inc(o_ready, 1)
                    if j + 1 < PAIRS or t == HEADS - 1:
                        step(n)
                        n += 1
                out_stage(n - 1, nn + 1, WO_KBS, 1.0, UNIT, first_split=True)

            def window_q_lo(j):
                dve.wait_ge(w_q_hi_ready, j + 1)
                for par in range(2):
                    own = slice(64 * par, 64 * par + 64)
                    last = dve.scalar_tensor_tensor(out=window_q(wide_lo, 0, par, j), in0=chunks(scaled[own, :]),
                                                    scalar=bq_scaled[own, j:j + 1],
                                                    in1=f32(window_q(wide_hi, par, par, j)),
                                                    op0=ALU.add, op1=ALU.subtract)
                last.then_inc(w_q_ready, 1)

            def window_k_lo(g):
                dve.wait_ge(w_k_hi_ready, g + 1)
                own, a = slice(64 * g, 64 * g + 64), K_AT + g * SEQ
                dve.scalar_tensor_tensor(out=wide_hi[64:128, a:a + SEQ], in0=sq[own, 1, :], scalar=bk[own, :],
                                         in1=f32((wide_lo if g else wide_hi)[own, a:a + SEQ]),
                                         op0=ALU.add, op1=ALU.subtract).then_inc(w_k_ready, 1)

            def window_v_lo():
                dve.wait_ge(w_v_hi_ready, 1)
                dve.tensor_tensor(wide_lo[:, V_AT:V_AT + SEQ], bank[7][:, :], f32(wide_hi[:, V_AT:V_AT + SEQ]),
                                  ALU.subtract).then_inc(w_v_ready, 1)
                dve.wait_ge(w_v_ready, 1)
                dve.wait_ge(v_moved_hi, 1)
                dve.tensor_copy(wide_lo[0:64, VS_AT:VS_AT + 3 * P], f32(wide_lo[64:128, V_AT:V_AT + 3 * P]))
                dve.tensor_copy(wide_lo[64:128, VS_AT:VS_AT + 3 * P], f32(wide_lo[0:64, V_AT + P:V_AT + 4 * P]))\
                   .then_inc(v_moved, 1)

            def window(nn):
                n = SWA_BASE
                for _ in range(2):
                    step(n)
                    n += 1
                mean_squares(nn, 5)
                diagonals(nn)
                dve.wait_ge(biases_ready, 1)
                dve.wait_ge(row_ready, nn + 1)

                def project_scaled(n, j):
                    if j:
                        dve.wait_ge(w_q_copied, j)
                        dve.wait_ge(w_q_ready, j)
                    dve.wait_ge(unit_used, n + 1)
                    dve.scalar_tensor_tensor(out=scaled, in0=bank[j % 2][:, :], scalar=QSCALE, in1=rstd_row[:, :],
                                             op0=ALU.mult, op1=ALU.mult).then_inc(w_q_scaled, 1)

                dve.tensor_tensor(sq[:, 1, :], bank[1][:, :], rstd_row[:, :], ALU.mult).then_inc(w_k_scaled, 1)
                project_scaled(n, 0)
                dve.tensor_tensor(sq[:, 0, :], bank[2][:, :], rstd_row[:, :], ALU.mult).then_inc(w_v_scaled, 1)
                window_k_lo(0)
                window_q_lo(0)
                dve.wait_ge(w_v_scaled, 1)
                dve.tensor_scalar(sq[:, 0, :], sq[:, 0, :], bv[:, 0:1], None, ALU.add).then_inc(w_v_biased, 1)
                step(n)
                n += 1

                for j in range(PAIRS + 1):
                    b = j % 2

                    def row_max(half):
                        if half == 0 and j >= 2:
                            dve.wait_ge(w_esink_ready, j - 1)
                        dve.wait_ge(w_scored, 2 * j + half + 1)
                        part = wmax[:, b, HALF * half:HALF * (half + 1)]
                        dve.tensor_reduce(part, bank[2 + half][:, :].rearrange("p (n k) -> p n k", k=P),
                                          AX_X, ALU.max, negate=True).then_inc(w_maxed, 1)
                        dve.wait_ge(w_maxed, 2 * j + half + 1)
                        dve.tensor_scalar(part, part, nsink[:, j:j + 1], None, ALU.min).then_inc(w_nmax_ready, 1)

                    def pt_lo(half):
                        a = PT_AT + half * SEQ
                        dve.wait_ge(w_pt_hi_ready, 2 * (j - 1) + half + 1)
                        dve.tensor_tensor(wide_lo[:, a:a + SEQ], bank[4 + half][:, :], f32(wide_hi[:, a:a + SEQ]),
                                          ALU.subtract).then_inc(w_pt_ready, 1)

                    def o_lo(j, half):
                        a = O_AT + j * SEQ + half * HALF * CHUNK
                        dve.wait_ge(w_o_hi_ready, 2 * j + half + 1)
                        for par in range(2):
                            rows = slice(64 * par, 64 * par + 64)
                            last = dve.tensor_tensor(chunks(wide_lo[rows, a:a + HALF * CHUNK]),
                                                     pair_output(bank[6 + half], par),
                                                     chunks(f32(wide_hi[rows, a:a + HALF * CHUNK])), ALU.subtract)
                        last.then_inc(w_o_ready, 1)

                    if j < PAIRS:
                        row_max(0)
                    if j + 1 < PAIRS:
                        project_scaled(n, j + 1)
                    if j:
                        pt_lo(0)
                    if j >= 2:
                        o_lo(j - 2, 0)
                    if j < PAIRS:
                        row_max(1)
                    if j >= 2:
                        o_lo(j - 2, 1)
                    if j:
                        pt_lo(1)
                    if j + 1 < PAIRS:
                        window_q_lo(j + 1)
                    if j < PAIRS:
                        dve.wait_ge(w_expd, CHUNKS * (j + 1))
                        dve.wait_ge(w_esink_ready, j + 1)
                        dve.tensor_tensor(wsum[:, b, :], wsum[:, b, :], esink[:, b, :], ALU.add)\
                           .then_inc(w_sum_ready, 1)
                        dve.wait_ge(w_sum_ready, j + 1)
                        dve.reciprocal(wrsum[:, b, :], wsum[:, b, :]).then_inc(w_rsum_ready, 1)
                        dve.wait_ge(w_rsum_ready, j + 1)
                        part = wprob[b].rearrange("p (n k) -> p n k", k=P)
                        dve.tensor_tensor(part, part, wrsum[:, b, :].unsqueeze(2).to_broadcast([P, CHUNKS, P]),
                                          ALU.mult).then_inc(w_p_ready, 1)
                        step(n)
                        n += 1
                    if j == 0:
                        window_v_lo()
                    if j == 2:
                        window_k_lo(1)
                for half in range(2):
                    o_lo(PAIRS - 1, half)
                out_stage(n - 1, nn + 1, WO_KBS, 1.0, UNIT, first_split=True)

            ffn(0, 0, False)
            fox(1)
            ffn(1, 2, False)
            ffn(2, 3, False)
            window(4)
            ffn(3, 5, True)
            mean_squares(6, 7)
            dve.wait_ge(rstd_ready, 7)
            for n in range(0, 2 * TB, 2):
                t = n % TB
                dve.wait_ge(y_turned, n + 1)
                dve.tensor_scalar(raw[:, n // 2, 0:512], bank[n][:, :], rstd[:, t:t + 1], None, ALU.mult)\
                   .then_inc(y_scaled_dve, 1)


def lay_out(inputs):
    a = {k: np.asarray(v) for k, v in inputs.items()}
    kb, pad = KB, np.zeros

    def columns(w, n):
        return w.reshape(kb, P, n, P).transpose(2, 1, 0, 3).reshape(n, P, UNIT)

    def wo(w):
        return w.reshape(2, 4, P, KB // 2, 256).transpose(3, 0, 2, 1, 4).reshape(WO_UNITS, P, UNIT)

    w_in = a["ffn_w_in"].reshape(4, 2, 4, P, 2, IN_BODIES, 256)
    ffn_in = w_in.transpose(0, 5, 4, 1, 3, 2, 6).reshape(4, IN_BODIES, IN_UNITS, P, UNIT)
    w_out = a["ffn_w_out"].reshape(4, FB, P, KB // 2, 256).transpose(0, 3, 2, 1, 4)
    ffn_out = pad((4, KB // 2, len(OUT_KBS), P, 3, 256), w_out.dtype)
    for u, kbs in enumerate(OUT_KBS):
        ffn_out[:, :, u, :, 0:len(kbs)] = w_out[:, :, :, kbs[0]:kbs[-1] + 1]
    ffn_out = ffn_out.reshape(4, KB // 2 * len(OUT_KBS) // RAW, RAW, P, OUT_COLS)

    fox = a["fox_w_in"][0]
    w_f = pad((1, P, UNIT), fox.dtype)
    w_f[0, :, 0:kb * HEADS] = fox[:, 3 * D:].reshape(kb, P, HEADS).transpose(1, 0, 2).reshape(P, kb * HEADS)
    w_v = fox[:, 2 * D:3 * D].reshape(4, 2, P, 2, 512).transpose(3, 0, 2, 1, 4).reshape(V_UNITS, P, UNIT)
    qk = np.stack([columns(fox[:, 0:D], PAIRS), columns(fox[:, D:2 * D], PAIRS)], 1).reshape(2 * PAIRS, P, UNIT)
    swa = a["swa_w_in"][0]
    kv = columns(swa[:, D:D + 2 * P], 2)
    mix_w = np.concatenate([w_v[0:1], w_f, w_v[1:], qk, wo(a["fox_w_o"][0]),
                            kv, columns(swa[:, 0:D], PAIRS), wo(a["swa_w_o"][0])])
    b = a["swa_b_in"][0]
    return {
        "x": a["x"].reshape(SEQ, D),
        "gains": np.concatenate([a["norm_g"].reshape(6, D), a["final_g"].reshape(1, D)]).reshape(7 * KB, P).T,
        "ffn_in": ffn_in,
        "ffn_out": ffn_out,
        "mix_w": mix_w,
        "fox_b": a["fox_b_f"].reshape(HEADS, 1),
        "swa_bq": b[0:D].reshape(PAIRS, P).transpose(1, 0),
        "swa_bk": b[D:D + P].reshape(P, 1),
        "swa_bv": b[D + P:D + 2 * P].reshape(P, 1),
        "sinks": a["swa_sinks"].reshape(PAIRS, 2).transpose(1, 0),
    }


def kernel(**inputs):
    import concourse.bacc as bacc
    from concourse.bass_utils import run_bass_kernel_spmd

    nc = bacc.Bacc("TRN2", target_bir_lowering=False, num_devices=1)
    arrays = {k: np.ascontiguousarray(v) for k, v in lay_out(inputs).items()}
    args = {k: nc.dram_tensor(k + "_dram", v.shape, mybir.dt.from_np(v.dtype), kind="ExternalInput").ap()
            for k, v in arrays.items()}
    y = nc.dram_tensor("y_dram", (SEQ, D), F32, kind="ExternalOutput").ap()
    build(nc, y=y, **args)
    r = run_bass_kernel_spmd(nc, [{k + "_dram": v for k, v in arrays.items()}], core_ids=[0])
    return r.results[0]["y_dram"].reshape(1, SEQ, D)
```
